# Optimizing a Trainium2 kernel written in Bass

```python
import jax, jax.numpy as jnp
from jax import lax
import numpy as np

D_MODEL = 2048
BATCH = 1
SEQ = 256
DEPTH = 1

HEAD_DIM = 64
N_Q_HEADS = 16
N_KV_HEADS = 4
ATTN_WIDTH = N_Q_HEADS * HEAD_DIM
KV_WIDTH = N_KV_HEADS * HEAD_DIM
WINDOW = 128
BLOCK = 128

RWKV_HEAD = 64
N_RWKV_HEADS = 16
RWKV_WIDTH = N_RWKV_HEADS * RWKV_HEAD
DECAY_LORA = 64
AAA_LORA = 64
MV_LORA = 32
GATE_LORA = 160
RWKV_GN_EPS = 64e-5

ATTN_COLS = ATTN_WIDTH + 2 * KV_WIDTH
SHIFT_WIDTH = 3 * RWKV_WIDTH + DECAY_LORA + AAA_LORA + GATE_LORA
IN_WIDTH = ATTN_COLS + SHIFT_WIDTH + 2 * D_MODEL

N_GROUPS = 4
EXPERTS_PER_GROUP = 8
N_EXPERTS = N_GROUPS * EXPERTS_PER_GROUP
TOP_K = 2
EXPERT_HIDDEN = D_MODEL // 4
MOE_BLOCK = 128

NORM_EPS = 1e-5

kernel_name = "hybrid_swa_rwkv7_hmoe"

def rms_norm(x, w):
    xf = x.astype(jnp.float32)
    y = xf * lax.rsqrt(jnp.mean(xf * xf, axis=-1, keepdims=True) + NORM_EPS)
    return (y * w.astype(jnp.float32)).astype(x.dtype)

def token_shift(z):
    return jnp.pad(z[:, :-1], ((0, 0), (1, 0), (0, 0)))

def _split(z, sizes):
    out, off = [], 0
    for s in sizes:
        out.append(z[..., off:off + s])
        off += s
    return out

def alibi_slopes(n):
    return jnp.exp2(-8.0 * jnp.arange(1, n + 1, dtype=jnp.float32) / n)

def sliding_window_attention(q, k, v, sinks):
    B, T = q.shape[:2]
    nb = T // BLOCK
    G = N_Q_HEADS // N_KV_HEADS
    f32 = jnp.float32
    qb = q.reshape(B, nb, BLOCK, N_KV_HEADS, G, HEAD_DIM).astype(f32)

    def with_prev(z):
        zb = z.reshape(B, nb, BLOCK, N_KV_HEADS, HEAD_DIM)
        prev = jnp.pad(zb[:, :-1], ((0, 0), (1, 0), (0, 0), (0, 0), (0, 0)))
        return jnp.concatenate([prev, zb], axis=2).astype(f32)

    kw, vw = with_prev(k), with_prev(v)
    scores = jnp.einsum('bnqhgd,bnkhd->bnhgqk', qb, kw) * (HEAD_DIM ** -0.5)
    qi = jnp.arange(BLOCK)[:, None]
    kj = jnp.arange(2 * BLOCK)[None, :]
    dist = qi + BLOCK - kj
    key_pos = (jnp.arange(nb)[:, None, None] - 1) * BLOCK + kj
    valid = (dist >= 0) & (dist < WINDOW) & (key_pos >= 0)
    slopes = alibi_slopes(N_Q_HEADS).reshape(N_KV_HEADS, G)[:, :, None, None]
    scores = scores - slopes * dist.astype(f32)
    scores = jnp.where(valid[None, :, None, None], scores, -jnp.inf)
    sink = sinks.astype(f32).reshape(N_KV_HEADS, G)[:, :, None, None]
    m = jnp.maximum(jnp.max(scores, axis=-1, keepdims=True), sink)
    p = jnp.exp(scores - m)
    probs = p / (jnp.sum(p, axis=-1, keepdims=True) + jnp.exp(sink - m))
    out = jnp.einsum('bnhgqk,bnkhd->bnqhgd', probs, vw)
    return out.reshape(B, T, ATTN_WIDTH)

def rwkv7_scan(r, decay, k, v, kk, a):
    B, T, H, N = r.shape

    def step(S, inp):
        r_t, w_t, k_t, v_t, kk_t, a_t = inp
        sa = jnp.einsum('bhvk,bhk->bhv', S, -kk_t)
        S = S * w_t[:, :, None, :] + sa[..., None] * (kk_t * a_t)[:, :, None, :] \
            + v_t[..., None] * k_t[:, :, None, :]
        return S, jnp.einsum('bhvk,bhk->bhv', S, r_t)

    xs = tuple(jnp.moveaxis(z, 1, 0) for z in (r, decay, k, v, kk, a))
    S0 = jnp.zeros((B, H, N, N), jnp.float32)
    _, ys = lax.scan(step, S0, xs)
    return jnp.moveaxis(ys, 0, 1)

def hybrid_mixer(h, v_first, w_in, shift_mix, attn_sinks, w0, w_up, a0, a_up, g_up,
                 k_k, k_a, r_k, ln_w, ln_b, w_branch_a, w_branch_b, w_out, vres):
    B, T, _ = h.shape
    f32 = jnp.float32
    proj = jnp.einsum('btd,dc->btc', h, w_in)
    q, k, v, z, gates = _split(proj, (ATTN_WIDTH, KV_WIDTH, KV_WIDTH, SHIFT_WIDTH, 2 * D_MODEL))

    attn = sliding_window_attention(q.reshape(B, T, N_Q_HEADS, HEAD_DIM),
                                    k.reshape(B, T, N_KV_HEADS, HEAD_DIM),
                                    v.reshape(B, T, N_KV_HEADS, HEAD_DIM), attn_sinks)

    z = (z + (token_shift(z) - z) * shift_mix).astype(f32)
    r, kr, vr, wd, ad, gd = _split(z, (RWKV_WIDTH, RWKV_WIDTH, RWKV_WIDTH, DECAY_LORA, AAA_LORA, GATE_LORA))
    w_log = -jax.nn.softplus(-(w0.astype(f32) + jnp.tanh(wd) @ w_up.astype(f32))) - 0.5
    a = jax.nn.sigmoid(a0.astype(f32) + ad @ a_up.astype(f32))
    g = jax.nn.sigmoid(gd) @ g_up.astype(f32)
    if vres is None:
        v_first = vr
    else:
        vd, vmix, vup, v0 = vres
        zv = h @ vd
        zv = (zv + (token_shift(zv) - zv) * vmix).astype(f32)
        vr = vr + (v_first - vr) * jax.nn.sigmoid(v0.astype(f32) + zv @ vup.astype(f32))

    def heads(t):
        return t.reshape(B, T, N_RWKV_HEADS, RWKV_HEAD)

    kk = heads(kr * k_k.astype(f32))
    kk = kk / jnp.maximum(jnp.sqrt(jnp.sum(kk * kk, axis=-1, keepdims=True)), 1e-12)
    kr = kr * (1.0 + (a - 1.0) * k_a.astype(f32))
    rh, kh, vh, ah = heads(r), heads(kr), heads(vr), heads(a)
    decay = heads(jnp.exp(-jnp.exp(w_log)))
    y = rwkv7_scan(rh, decay, kh, vh, kk, ah)
    mu = jnp.mean(y, axis=-1, keepdims=True)
    var = jnp.mean(jnp.square(y - mu), axis=-1, keepdims=True)
    y = ((y - mu) * lax.rsqrt(var + RWKV_GN_EPS)).reshape(B, T, RWKV_WIDTH)
    y = y * ln_w.astype(f32) + ln_b.astype(f32)
    bonus = jnp.sum(rh * kh * r_k.astype(f32), axis=-1, keepdims=True) * vh
    y = (y + bonus.reshape(B, T, RWKV_WIDTH)) * g

    ga, gb = _split(gates, (D_MODEL, D_MODEL))
    merged = jax.nn.sigmoid(ga) * (attn.astype(h.dtype) @ w_branch_a) \
        + jax.nn.sigmoid(gb) * (y.astype(h.dtype) @ w_branch_b)
    return merged @ w_out, v_first

def hierarchical_moe(h, rg_w, rg_b, re_w, re_b, w_gate, w_up, w_down):
    B, T, D = h.shape
    N = B * T
    f32 = jnp.float32
    xt = h.reshape(N, D)
    glog = (xt @ rg_w).astype(f32) + rg_b.astype(f32)
    gprob = jax.nn.softmax(glog, axis=-1)
    gsel = jnp.argmax(glog, axis=-1)
    gp = jnp.take_along_axis(gprob, gsel[:, None], axis=-1)
    elog = ((xt @ re_w).astype(f32) + re_b.astype(f32)).reshape(N, N_GROUPS, EXPERTS_PER_GROUP)
    elog_g = jnp.take_along_axis(elog, gsel[:, None, None], axis=1)[:, 0]
    top_vals, top_idx = lax.top_k(elog_g, TOP_K)
    ew = jax.nn.softmax(top_vals, axis=-1) * gp

    expert_ids = (gsel[:, None] * EXPERTS_PER_GROUP + top_idx).reshape(-1)
    token_ids = jnp.repeat(jnp.arange(N, dtype=jnp.int32), TOP_K)
    weights = ew.reshape(-1)
    A = N * TOP_K
    n_blocks = -(-A // MOE_BLOCK) + N_EXPERTS
    cap = n_blocks * MOE_BLOCK

    order = jnp.argsort(expert_ids)
    se = expert_ids[order]
    counts = jnp.bincount(expert_ids, length=N_EXPERTS)
    starts = jnp.cumsum(counts) - counts
    padded = (counts + MOE_BLOCK - 1) // MOE_BLOCK * MOE_BLOCK
    pad_ends = jnp.cumsum(padded)
    pad_starts = pad_ends - padded
    dest = pad_starts[se] + (jnp.arange(A) - starts[se])
    slot_tok = jnp.full((cap,), N, jnp.int32).at[dest].set(token_ids[order])
    slot_w = jnp.zeros((cap,), f32).at[dest].set(weights[order])
    block_expert = jnp.minimum(
        jnp.searchsorted(pad_ends, jnp.arange(n_blocks) * MOE_BLOCK, side='right'), N_EXPERTS - 1)

    x_pad = jnp.concatenate([xt, jnp.zeros((1, D), xt.dtype)], axis=0)
    xb = x_pad[slot_tok].reshape(n_blocks, MOE_BLOCK, D)

    def expert_block(args):
        xblk, e = args
        hid = jax.nn.silu(xblk @ w_gate[e]) * (xblk @ w_up[e])
        return hid @ w_down[e]

    yb = lax.map(expert_block, (xb, block_expert)).reshape(cap, D).astype(f32)
    y = jnp.zeros((N + 1, D), f32).at[slot_tok].add(yb * slot_w[:, None])
    return y[:N].reshape(B, T, D).astype(h.dtype)

def setup_inputs(seed: int = 0) -> dict:
    key = jax.random.key(seed)
    ks = iter(jax.random.split(key, 40))
    f32 = jnp.float32

    def nrm(shape, scale):
        return jax.random.normal(next(ks), shape, f32) * scale

    def uni(shape):
        return jax.random.uniform(next(ks), shape, f32)

    L, Lv = DEPTH, DEPTH - 1
    return {
        "x": nrm((BATCH, SEQ, D_MODEL), 1.0),
        "attn_norm_w": 1.0 + nrm((L, D_MODEL), 0.02),
        "w_in": nrm((L, D_MODEL, IN_WIDTH), D_MODEL ** -0.5),
        "shift_mix": uni((L, SHIFT_WIDTH)),
        "attn_sinks": nrm((L, N_Q_HEADS), 0.5),
        "rwkv_w0": nrm((L, RWKV_WIDTH), 1.0) - 0.5,
        "rwkv_w_up": nrm((L, DECAY_LORA, RWKV_WIDTH), 0.5 * DECAY_LORA ** -0.5),
        "rwkv_a0": nrm((L, RWKV_WIDTH), 0.5),
        "rwkv_a_up": nrm((L, AAA_LORA, RWKV_WIDTH), 0.5 * AAA_LORA ** -0.5),
        "rwkv_g_up": nrm((L, GATE_LORA, RWKV_WIDTH), GATE_LORA ** -0.5),
        "rwkv_k_k": 0.85 + nrm((L, RWKV_WIDTH), 0.05),
        "rwkv_k_a": 1.0 + nrm((L, RWKV_WIDTH), 0.05),
        "rwkv_r_k": nrm((L, N_RWKV_HEADS, RWKV_HEAD), 0.1),
        "rwkv_ln_w": 1.0 + nrm((L, RWKV_WIDTH), 0.02),
        "rwkv_ln_b": nrm((L, RWKV_WIDTH), 0.02),
        "vres_down": nrm((Lv, D_MODEL, MV_LORA), D_MODEL ** -0.5),
        "vres_mix": uni((Lv, MV_LORA)),
        "vres_up": nrm((Lv, MV_LORA, RWKV_WIDTH), 0.5 * MV_LORA ** -0.5),
        "vres_v0": nrm((Lv, RWKV_WIDTH), 0.5),
        "w_branch_a": nrm((L, ATTN_WIDTH, D_MODEL), ATTN_WIDTH ** -0.5),
        "w_branch_b": nrm((L, RWKV_WIDTH, D_MODEL), RWKV_WIDTH ** -0.5),
        "w_out": nrm((L, D_MODEL, D_MODEL), D_MODEL ** -0.5),
        "ffn_norm_w": 1.0 + nrm((L, D_MODEL), 0.02),
        "router_group_w": nrm((L, D_MODEL, N_GROUPS), D_MODEL ** -0.5),
        "router_group_b": nrm((L, N_GROUPS), 0.01),
        "router_expert_w": nrm((L, D_MODEL, N_EXPERTS), D_MODEL ** -0.5),
        "router_expert_b": nrm((L, N_EXPERTS), 0.01),
        "expert_w_gate": nrm((L, N_EXPERTS, D_MODEL, EXPERT_HIDDEN), D_MODEL ** -0.5),
        "expert_w_up": nrm((L, N_EXPERTS, D_MODEL, EXPERT_HIDDEN), D_MODEL ** -0.5),
        "expert_w_down": nrm((L, N_EXPERTS, EXPERT_HIDDEN, D_MODEL), EXPERT_HIDDEN ** -0.5),
        "final_norm_w": 1.0 + nrm((D_MODEL,), 0.02),
    }

def reference(x, attn_norm_w, w_in, shift_mix, attn_sinks, rwkv_w0, rwkv_w_up, rwkv_a0,
              rwkv_a_up, rwkv_g_up, rwkv_k_k, rwkv_k_a, rwkv_r_k, rwkv_ln_w, rwkv_ln_b,
              vres_down, vres_mix, vres_up, vres_v0, w_branch_a, w_branch_b, w_out,
              ffn_norm_w, router_group_w, router_group_b, router_expert_w, router_expert_b,
              expert_w_gate, expert_w_up, expert_w_down, final_norm_w):
    v_first = None
    for i in range(DEPTH):
        vres = None if i == 0 else (vres_down[i - 1], vres_mix[i - 1], vres_up[i - 1], vres_v0[i - 1])
        h = rms_norm(x, attn_norm_w[i])
        mix, v_first = hybrid_mixer(h, v_first, w_in[i], shift_mix[i], attn_sinks[i],
                                    rwkv_w0[i], rwkv_w_up[i], rwkv_a0[i], rwkv_a_up[i], rwkv_g_up[i],
                                    rwkv_k_k[i], rwkv_k_a[i], rwkv_r_k[i], rwkv_ln_w[i], rwkv_ln_b[i],
                                    w_branch_a[i], w_branch_b[i], w_out[i], vres)
        x = x + mix.astype(x.dtype)
        hf = rms_norm(x, ffn_norm_w[i])
        x = x + hierarchical_moe(hf, router_group_w[i], router_group_b[i], router_expert_w[i],
                                 router_expert_b[i], expert_w_gate[i], expert_w_up[i],
                                 expert_w_down[i]).astype(x.dtype)
    return rms_norm(x, final_norm_w)


_drawn_inputs = setup_inputs


def setup_inputs(seed=0):
    import zlib

    import numpy as np

    out = dict(_drawn_inputs(seed))
    spreads = {}
    factors = {'attn_sinks': 3.33,
     'rwkv_k_k': 6.317,
     'rwkv_ln_w': 4.697,
     'rwkv_ln_b': 3.68,
     'router_group_b': 4.63,
     'router_expert_b': 6.68,
     'final_norm_w': 2.767}
    for name, (base, spread) in spreads.items():
        noise = np.random.default_rng([zlib.crc32(name.encode()), seed]).standard_normal(out[name].shape)
        drawn = base * np.exp(spread * noise) if base else spread * noise
        out[name] = __import__('jax').numpy.asarray(drawn.astype(out[name].dtype))
    for name, factor in factors.items():
        out[name] = (out[name] * factor).astype(out[name].dtype)
    return out
```

```python
import concourse.bass as bass
from concourse import mybir
from contextlib import ExitStack

F32 = mybir.dt.float32
F32R = mybir.dt.float32r
I32 = mybir.dt.int32
ALU = mybir.AluOpType
ACT = mybir.ActivationFunctionType
AX = mybir.AxisListType

P = 128
TOK = 256
TT = TOK // P
D = 2048
KT = D // P
HD = 64
QH, KVH = 16, 4
RW = 1024
RCT = RW // P
HALVES = 2
HJ = RCT // HALVES
LORA = 64
GLORA = 160
NEXP, NGRP, EPG = 32, 4, 8
HID = 512
GE = 4
CAP = 32
GROUPS = NEXP // GE
ATTN_W, KV_W = QH * HD, KVH * HD
Z0 = ATTN_W + 2 * KV_W
LORA0 = Z0 + 3 * RW
LORA_W = 2 * LORA + GLORA
GA0 = LORA0 + LORA_W
GB0 = GA0 + D
NORM_EPS = 1e-5
GN_EPS = 64e-5
DECAY_C = -0.6065306597126334
BIG = 1e30

SLOT = 4096
RING = 4

LAG = 3

VEC_ROWS = (("anorm", 16), ("mix", 27), ("k_k", 8), ("k_a", 8), ("r_k", 8), ("a0", 8),
            ("ln_w", 8), ("ln_b", 8))
VEC = {}
_at = 0
for _name, _n in VEC_ROWS:
    VEC[_name] = _at
    _at += _n
NVEC = _at

CONST_COLS = (("ident", 128), ("tri", 256), ("upper", 128), ("ones", 128), ("blk", 128), ("mU", 64), ("mUi", 64),
              ("lvlT", 384), ("m1L", 64), ("eye", 64), ("dist", 256), ("iota", 32))
CC = {}
_at = 0
for _name, _n in CONST_COLS:
    CC[_name] = _at
    _at += _n
NCONST = _at


def constants():
    import numpy as np
    p = np.arange(P)[:, None]
    c = np.arange(P)[None, :]
    t = p % HD
    x = np.arange(HD)[None, :]
    out = np.zeros((P, NCONST), np.float32)

    def put(name, a):
        out[:, CC[name]:CC[name] + a.shape[1]] = a

    same = (p // HD) == (c // HD)
    put("ident", p == c)
    put("tri", np.concatenate([same & (p <= c), same & (p < c)], 1))
    put("upper", p < c)
    put("ones", np.ones((P, P)))
    put("blk", same)
    put("mU", t < x)
    put("mUi", t <= x)
    lv = [(t < x) & (t // (2 * b) == x // (2 * b)) & (t // b != x // b) for b in (1, 2, 4, 8, 16, 32)]
    put("lvlT", np.concatenate(lv, 1))
    put("m1L", (x < t) & (t // 2 == x // 2))
    put("eye", t == x)
    put("dist", np.concatenate([np.where(c > p, p + P - c, BIG), np.where(c <= p, p - c, BIG)], 1))
    put("iota", np.broadcast_to(np.arange(CAP)[None, :], (P, CAP)))
    return out


class Steps:

    def __init__(self, sem):
        self.sem, self.n, self.base = sem, 0, 0

    def on(self, ins):
        ins.then_inc(self.sem, 1)
        self.n += 1

    def last(self, eng):
        eng.wait_ge(self.sem, self.base + self.n)

    def enter(self, i, per):
        self.start, self.per = self.n, per
        self.base, self.n = self.start + i * per, 0

    def leave(self, count):
        assert self.n == self.per, (self.n, self.per)
        self.base, self.n = 0, self.start + count * self.per


def hybrid_layer(nc, a, out):
    with ExitStack() as ctx:
        def sb(name, shape, dt=F32):
            return ctx.enter_context(nc.sbuf_tensor(name, shape, dt))

        sems = {}

        def S(name):
            if name not in sems:
                sems[name] = ctx.enter_context(nc.semaphore(name))
            return sems[name]

        ring = sb("ring", [P, RING, SLOT])
        cst = sb("cst", [P, NCONST])
        vrow = sb("vrow", [P, P])
        vecT = sb("vecT", [P, P])
        fnorm = sb("fnorm", [P, KT])
        omm = sb("omm", [P, 27])
        omka = sb("omka", [P, 8])
        sink = sb("sink", [P, QH])
        nsm = sb("nsm", [P, 8])
        rstd = sb("rstd", [P, 6])
        amax = sb("amax", [P, 8])
        aes = sb("aes", [P, 8])
        asum = sb("asum", [P, 8])
        pend = sb("pend", [P, 16])
        gn = sb("gn", [P, 3, 16])
        flag = sb("flag", [1, 1], I32)
        rbias = sb("rbias", [P, 36])
        rs = sb("rs", [P, 1280])
        ps = ctx.enter_context(nc.psum_tensor("ps", [P, 8, 512], F32))

        with ExitStack() as early:
            def over(name, shape, dt=F32R):
                return early.enter_context(nc.sbuf_tensor(name, shape, dt))

            over("below", [P, 15104], F32)
            w3 = [over(f"w_{x}", [P, 3, 1024]) for x in ("hi", "lo")]
            w1 = [over(f"w4_{x}", [P, 1, 1024]) for x in ("hi", "lo")]
            over("between", [P, 1024], F32)
            h_hi, h_lo = (over(f"h_{x}", [P, KT, TOK]) for x in ("hi", "lo"))
        arena = sb("arena", [P, 17152 + 15360])

        def C(name, n=None, at=0):
            w = dict(CONST_COLS)[name]
            return cst[:, CC[name] + at:CC[name] + at + (n or w)]

        def vec(name, i=0, n=1):
            if name == "fnorm":
                return fnorm[:, i:i + n]
            return vecT[:, VEC[name] + i:VEC[name] + i + n]

        def A(at, n):
            return arena[:, at:at + n]

        def rep(ap, n):
            return ap.unsqueeze(2).to_broadcast([ap.shape[0], ap.shape[1], n])

        def tile16(ap):
            return ap.unsqueeze(1).to_broadcast([P, 16, 64])

        HT, ZB, LZ0, LW0, AT0, T0 = 0, 4096, 10240, 11008, 15104, 17152
        hT = A(HT, 4096).rearrange("p (k t) -> p k t", k=KT)
        zT = A(ZB, 6144).rearrange("p (c t) -> p c t", c=24)
        lz = A(LZ0, 768).rearrange("p (c t) -> p c t", c=3)
        wua, g1w, g2w, w0row = (A(LW0 + 1024 * i, 1024) for i in range(4))
        attnT = A(AT0, 2048).rearrange("p (c t) -> p c t", c=8)
        yT = zT[:, 16:24, :]

        def U(i, n=1):
            return A(T0 + 1024 * i, 1024 * n)

        x_sb = U(4, 4).rearrange("p (a d) -> p a d", a=TT)
        xn = U(0, 4).rearrange("p (a d) -> p a d", a=TT)
        junk = U(0, 4).rearrange("p (a d) -> p a d", a=TT)
        probs = U(0, 2).rearrange("p (h k) -> p h k", h=8)
        probsT = U(2, 2).rearrange("p (b h q) -> p b h q", b=2, h=8)
        qT = U(4, 2).rearrange("p (c t) -> p c t", c=8)
        kTa = A(T0 + 6144, 512).rearrange("p (c t) -> p c t", c=2)
        vA = A(T0 + 6656, 512).rearrange("p (a c) -> p a c", a=TT)
        mg = U(0, 4).rearrange("p (a d) -> p a d", a=TT)
        mT = U(8, 4).rearrange("p (k t) -> p k t", k=KT)
        gates = [[A(LW0 + 1024 * (2 * b + g), 1024).rearrange("p (a n) -> p a n", a=TT) for g in range(2)] for b in range(2)]
        hfn = A(HT, 4096).rearrange("p (a d) -> p a d", a=TT)
        fout = hfn
        hfT = mT
        rw = A(T0 + 12288, 576).rearrange("p (k n) -> p k n", k=KT)
        junk2 = A(ZB, 4096).rearrange("p (a d) -> p a d", a=TT)
        XS = A(4096, 2048).rearrange("p (k s) -> p k s", k=KT)
        YS = A(6144, 2048)
        SG = A(8192, 512)
        HIDB = A(8704, 512)
        HIDT = A(9216, 512).rearrange("p (k s) -> p k s", k=4)
        OH = A(9728, 256)
        OHW = A(9984, 256)
        CTB = A(10240, 256)
        FW = A(10496, 2048)
        fSG, fHID, fHT = A(4096, 1024), A(5120, 1024), A(6144, 1024)

        gtmp = rs[:, 0:1024].rearrange("p (b n) -> p b n", b=2)
        gate_d = nc.dram_tensor("gate_spill", [P, TT, 2 * D], F32, kind="Internal").ap()
        w_in = a["w_in"][0]
        block = ctx.enter_context(nc.Block())

        def cols(c0, half, w):
            return w_in[:, c0:c0 + w].rearrange("(k p) n -> p k n", p=P)[:, 8 * half:8 * half + 8, :]

        def slot(n, w=512):
            return ring[:, n % RING, 0:8 * w].rearrange("p (k n) -> p k n", k=8)

        def pieces(b):
            return [(w1[x][:, 0, :] if b == 3 else w3[x][:, b, :]) for x in range(2)]

        def hf(x, k, t0=0, n=TOK):
            return (h_hi, h_lo)[x][:, k, t0:t0 + n]

        PRODUCTS = ((0, 0), (0, 1), (1, 0))
        UZ, UQ = 48, 24

        def z_piece(x):
            c, q = x // 4, x % 4
            return NZ + c, slot(NZ + c)[:, :, 128 * q:128 * q + 128]

        def q_piece(x):
            c, q = NQ + x // 4, x % 4
            if x < 16:
                return c, slot(c).rearrange("p k (a j n) -> p k a j n", a=2, j=4)[:, :, :, q, :], \
                    lambda o: o.rearrange("p (k a n) -> p k a n", k=8, a=2)
            if q < 2:
                return c, slot(c)[:, :, 128 * q:128 * q + 128], lambda o: o.rearrange("p (k n) -> p k n", k=8)
            return c, slot(c)[:, 4 * (q - 2):4 * (q - 2) + 4, KV_W:2 * KV_W], \
                lambda o: o.rearrange("p (k n) -> p k n", k=4)

        def q_buffer(x):
            return x % 3, 4 + UZ + x - 2 if x >= 3 else 4 + UZ - 4 + x + 1

        NZ = 2
        NQ = NZ + 12
        NG = NQ + 6
        NM = NG + 16
        NO = NM + 8
        NE = NO + 8
        PER_G = 24

        @block.sync
        def _(sp):
            def load(n, dst, src, turn=0, per=0):
                if per or n >= RING:
                    sp.wait_ge(S("chunk_used"), turn * per + (n - RING + 1))
                sp.dma_start(dst, src).then_inc(S(f"slot_full{n % RING}"), 16)

            for h in range(2):
                load(h, slot(h, LORA_W), cols(LORA0, h, LORA_W))
            zc = w_in.rearrange("(k p) n -> p k n", p=P)
            for c in range(4):
                load(NZ + c, slot(NZ + c), cols(Z0 + 512 * (c // 2), c % 2, 512))
            with sp.Fori(1, 3) as i:
                for c in range(4):
                    b, h = divmod(c, 2)
                    load(NZ + c, slot(NZ + c), zc[:, 8 * h:8 * h + 8, bass.ds(i * RW + (Z0 + 512 * b), 512)], turn=i, per=4)
            for c in range(6):
                load(NQ + c, slot(NQ + c), cols(512 * (c // 2), c % 2, 512))
            for c in range(16):
                load(NG + c, slot(NG + c), cols(GA0 + 512 * (c // 2), c % 2, 512))
            wa = a["w_branch_a"][0].rearrange("(k p) n -> p k n", p=P)
            wb = a["w_branch_b"][0].rearrange("(k p) n -> p k n", p=P)
            for c in range(8):
                load(NM + c, slot(NM + c), (wa, wb)[c % 2][:, :, 512 * (c // 2):512 * (c // 2) + 512])
            wo = a["w_out"][0].rearrange("(k p) n -> p k n", p=P)
            for c in range(8):
                load(NO + c, slot(NO + c), wo[:, 8 * (c % 2):8 * (c % 2) + 8, 512 * (c // 2):512 * (c // 2) + 512])
            eg = a["expert_w_gate"][0].rearrange("e (p k) h -> p e (k h)", p=P)
            eu = a["expert_w_up"][0].rearrange("e (p k) h -> p e (k h)", p=P)
            ed = a["expert_w_down"][0].rearrange("e (k p) n -> p e k n", p=P)
            with sp.Fori(0, GROUPS) as g:
                first = sp.snap(g * GE)
                for c in range(16):
                    n = NE + c
                    k = c // 2
                    sp.wait_ge(S("chunk_used"), g * PER_G + (n - RING + 1))
                    dst = ring[:, n % RING, :].rearrange("p (j n) -> p j n", j=GE)
                    src = (eu if c % 2 else eg)[:, bass.ds(first, GE), 2 * HID * k:2 * HID * (k + 1)]
                    sp.dma_start(dst, src).then_inc(S(f"slot_full{n % RING}"), 16)
                for c in range(8):
                    n = NE + 16 + c
                    kh, nh = divmod(c, 2)
                    sp.wait_ge(S("chunk_used"), g * PER_G + (n - RING + 1))
                    src = ed[:, bass.ds(first, GE), kh, 1024 * nh:1024 * nh + 1024]
                    sp.dma_start(ring[:, n % RING, :].rearrange("p (j n) -> p j n", j=GE), src)\
                        .then_inc(S(f"slot_full{n % RING}"), 16)
            sp.wait_ge(S("flag_set"), 1)
            over = sp.value_load(flag[0:1, 0:1], min_val=0, max_val=1)
            with sp.If(over > 0):
                sp.wait_ge(S("chunk_used"), NE + PER_G * GROUPS)
                with sp.Fori(0, NEXP) as e:
                    sp.wait_ge(S("fb_dn_ps"), e * 2 + 1)
                    for s in range(4):
                        w = (eg if s < 2 else eu)[:, bass.ds(e, 1), SLOT * (s % 2):SLOT * (s % 2) + SLOT]
                        sp.dma_start(ring[:, s, :], w.rearrange("p e n -> p (e n)")).then_inc(S("fb_up_in"), 16)
                    sp.wait_ge(S("fb_up_used"), e + 1)
                    for s in range(2):
                        w = ed[:, bass.ds(e, 1), 2 * s:2 * s + 2, :]
                        sp.dma_start(ring[:, s, :].rearrange("p (k n) -> p k n", k=2),
                                     w.rearrange("p e k n -> p (e k) n")).then_inc(S("fb_down_in"), 16)
                sp.nop()
            for t in range(TT):
                sp.wait_ge(S("fin"), t + 1)
                sp.dma_start(out[0].rearrange("(a p) d -> p a d", p=P)[:, t, :], fout[:, t, :]).then_inc(S("stored"), 16)
            sp.wait_ge(S("stored"), 16 * TT)

        @block.gpsimd
        def _(pool):
            pool.memset(vrow[:, :], 0.0).then_inc(S("vrow_zero"), 1)
            pool.wait_ge(S("const_in"), 16)
            for hh in range(HALVES):
                pool.wait_ge(S("lt_done"), hh + 1)
                for lv in range(1, 6):
                    if lv > 1:
                        pool.wait_ge(S("v1_ps"), 10 * hh + 2 * (lv - 1))
                    pool.tensor_tensor(U(6).rearrange("p (g x) -> p g x", g=16),
                                       U(8).rearrange("p (g x) -> p g x", g=16),
                                       tile16(C("lvlT", 64, 64 * lv)), ALU.mult).then_inc(S("ltm_done"), 1)

        @block.tensor
        def _(pe):
            mm = nc.tensor.matmul

            def full(n, turn=0, per=0):
                pe.wait_ge(S(f"slot_full{n % RING}"), turn * (16 * per // RING) + 16 * (n // RING + 1))

            def tp(o, i):
                return nc.tensor.transpose(o, i, C("ident")[0:i.shape[0], 0:i.shape[0]])

            def transposes(src, ev):
                for g in range(8):
                    t, kq = divmod(g, 4)
                    for q in range(4):
                        k = 4 * kq + q
                        last = tp(ps[:, g, 128 * q:128 * q + 128], src[:, t, 128 * k:128 * k + 128])
                    last.then_inc(S(ev), 1)

            pe.wait_ge(S("const_in"), 16)
            pe.wait_ge(S("vec_in"), 16 * 11)
            tp(ps[:, 0, 0:NVEC], vrow[0:NVEC, :]).then_inc(S("vt_ps"), 1)
            pe.wait_ge(S("vt_done"), 1)
            pe.wait_ge(S("xn_done"), 2)
            transposes(xn, "xt_ps")
            pe.wait_ge(S("ht_done"), 8)

            full(0)
            full(1)
            for t, m in enumerate((128, 128, 32)):
                for k in range(KT):
                    last = mm(ps[0:m, 4 + t, 0:TOK], slot(k // 8, LORA_W)[:, k % 8, 128 * t:128 * t + m], hT[:, k, :],
                              start=k == 0, stop=k == KT - 1)
                    if t == 2 and k % 8 == 7:
                        last.then_inc(S("chunk_used"), 1)
                if t < 2:
                    last.then_inc(S("z_ps"), 1)
            def unit(buf, out, ks, start, stop):
                hi, lo = pieces(buf)
                for n, k in enumerate(ks):
                    for p, (w, x) in enumerate(PRODUCTS):
                        last = mm(out, (hi, lo)[w][:, 128 * n:128 * n + 128], hf(x, k),
                                  start=start and n == 0 and p == 0, stop=stop and n == 7 and p == 2)
                return last

            pe.wait_ge(S("h_lo_done"), 1)
            with pe.Fori(0, 3) as i:
                for x in range(16):
                    b, h, c = x // 8, x // 4 % 2, x % 4
                    if x % 8 == 0:
                        pe.wait_ge(S("z_done"), i * 8 + (1 + 2 * b))
                    pe.wait_ge(S("w_lo"), i * 16 + (x + 1))
                    unit(x % 4, ps[:, 4 * b + c, 0:TOK], range(8 * h, 8 * h + 8), h == 0, h == 1)\
                        .then_inc(S("w_used"), 1)
            for x in range(UQ):
                c = x % 4
                b, h = divmod(x // 4, 2)
                if x in (0, 8):
                    pe.wait_ge(S("z_done"), (23, 27)[b])
                if x == 16:
                    pe.wait_ge(S("qkv_done"), 4)
                pe.wait_ge(S("w_lo"), UZ + x + 1)
                buf = q_buffer(x)[0]
                if b < 2 or c < 2:
                    last = unit(buf, ps[:, 4 * (b % 2) + c, 0:TOK], range(8 * h, 8 * h + 8), h == 0, h == 1)
                else:
                    for k in range(4):
                        kk = 8 * h + 4 * (c - 2) + k
                        for t in range(TT):
                            for p, (w, y) in enumerate(PRODUCTS):
                                last = mm(ps[:, 2 + t, 0:KV_W], hf(y, kk, 128 * t, 128),
                                          pieces(buf)[w][:, KV_W * k:KV_W * k + KV_W],
                                          start=kk == 0 and p == 0, stop=kk == KT - 1 and p == 2)
                last.then_inc(S("w_used"), 1)

            gate_part = [0]

            def gate_half():
                m = gate_part[0]
                gate_part[0] += 1
                b, t, h = m // 4, m // 2 % 2, m % 2
                if h == 0 and m:
                    pe.wait_ge(S("gate_out"), m // 2)
                full(NG + 2 * b + h)
                for k in range(8):
                    last = mm(ps[:, 7, :], hT[:, 8 * h + k, 128 * t:128 * t + 128], slot(NG + 2 * b + h)[:, k, :],
                              start=h == 0 and k == 0, stop=h == 1 and k == 7)
                if t:
                    last.then_inc(S("chunk_used"), 1)
                elif h:
                    last.then_inc(S("gate_ps"), 1)

            sc = ps[:, 0:4, :].rearrange("p b (j k) -> p (b j) k", j=2)
            pt = [ps[:, 4:6, :].rearrange("p b (h q) -> p (b h) q", h=4),
                  ps[:, 2:4, :].rearrange("p b (h q) -> p (b h) q", h=4)]
            pe.wait_ge(S("qkv_done"), 12)
            for u in range(4):
                n, hg = divmod(u, 2)
                if u:
                    pe.wait_ge(S("pv_done"), u)
                for j in range(4):
                    for hp in range(2):
                        r = slice(64 * hp, 64 * hp + 64)
                        last = mm(sc[:, 4 * hp + j, 0:128 * (n + 1)], qT[r, 4 * hg + j, 128 * n:128 * n + 128],
                                  kTa[r, hg, 0:128 * (n + 1)], start=True, stop=True)
                last.then_inc(S("sc_ps"), 1)
                gate_half()
                pe.wait_ge(S("pr_done"), u + 1)
                for kb in range(n + 1):
                    for h in range(8):
                        last = tp(pt[kb][:, h, :], probs[:, h, 128 * kb:128 * kb + 128])
                last.then_inc(S("pt_ps"), 1)
                gate_half()
                pe.wait_ge(S("pt_done"), (1, 2, 4, 6)[u])
                for h in range(8):
                    hp, j = divmod(h, 4)
                    kv = 2 * hg + hp
                    o = ps[64 * (j % 2):64 * (j % 2) + 64, 0, 128 * (2 * hp + j // 2):128 * (2 * hp + j // 2) + 128]
                    for kb in range(n + 1):
                        last = mm(o, vA[:, kb, 64 * kv:64 * kv + 64], probsT[:, kb, h, :], start=kb == 0, stop=kb == n)
                last.then_inc(S("pv_ps"), 1)

            def blk(ap, hp, ci, j, w=64):
                o = w * (8 * hp + 4 * ci + j)
                return ap[:, o:o + w]

            pairs = [(cp, hp, ci, j) for ci in range(2) for j in range(4) for hp in range(2) for cp in range(2)]
            quads = [(cp, ci, j) for ci in range(2) for j in range(4) for cp in range(2)]
            pe.wait_ge(S("lora_done"), 3)
            pe.wait_ge(S("small_in"), 16 * 7)
            for hh in range(HALVES):
                AR = U(0, 2).rearrange("p (j w t) -> p j w t", j=HJ, w=2)
                BT = U(2).rearrange("p (j t) -> p j t", j=HJ)
                KTT = U(3).rearrange("p (j t) -> p j t", j=HJ)
                MVA = U(4, 2)
                UA = U(12, 2)
                if hh:
                    pe.wait_ge(S("y_done"), hh)
                else:
                    pe.wait_ge(S("pv_done"), 4)
                hc = 512 * hh
                for t in range(TT):
                    mm(ps[:, t, :], lz[0:64, 0, 128 * t:128 * t + 128], wua[0:64, hc:hc + 512], start=True, stop=False)
                    last = mm(ps[:, t, :], C("ones")[0:1, :], w0row[0:1, hc:hc + 512], start=False, stop=True)
                last.then_inc(S("wl_ps"), 1)
                for j in range(HJ):
                    last = mm(ps[:, 2 + j // 2, 256 * (j % 2):256 * (j % 2) + 256],
                              wua[64:128, hc + 128 * j:hc + 128 * j + 128], lz[64:128, 0, :], start=True, stop=True)
                last.then_inc(S("a_ps"), 1)
                gate_half()
                pe.wait_ge(S("sg_done"), hh + 1)
                for j in range(HJ):
                    for t in range(TT):
                        last = mm(ps[:, (4, 5, 6, 0)[j], 256 * t:256 * t + 256],
                                  U(4)[:, 512 * t + 128 * j:512 * t + 128 * j + 128], C("tri"), start=True, stop=True)
                last.then_inc(S("cum_ps"), 1)
                pe.wait_ge(S("sq_done"), hh + 1)
                pe.wait_ge(S("a_done"), hh + 1)
                for b in range(2):
                    last = mm(ps[:, 1 + b, :], C("blk"), U(7)[:, 512 * b:512 * b + 512], start=True, stop=True)
                last.then_inc(S("ks_ps"), 1)
                gate_half()
                pe.wait_ge(S("nrm_done"), hh + 1)
                for ci in range(2):
                    for j in range(HJ):
                        last = tp(ps[:, 2 + ci, 128 * j:128 * j + 128], yT[:, HJ * hh + j, 128 * ci:128 * ci + 128])
                last.then_inc(S("vtr_ps"), 1)
                gate_half()
                pe.wait_ge(S("rk_done"), hh + 1)
                pe.wait_ge(S("P_done"), hh + 1)
                for b in range(2):
                    last = mm(ps[:, 4 + b, :], C("blk"), U(12)[:, 512 * b:512 * b + 512], start=True, stop=True)
                last.then_inc(S("bon_ps"), 1)
                gate_half()
                gate_half()

                def tk(ap, c):
                    return ap[:, 64 * c:64 * c + 64]

                pe.wait_ge(S("arbk"), hh + 1)
                pe.wait_ge(S("vt2_done"), hh + 1)
                pe.wait_ge(S("bon_done"), hh + 1)
                for cp, hp, ci, j in pairs:
                    r, q, c = slice(64 * hp, 64 * hp + 64), slice(64 * cp, 64 * cp + 64), 2 * ci + cp
                    last = mm(ps[q, hp, 256 * ci + 64 * j:256 * ci + 64 * j + 64], tk(AR[r, j, 0, :], c), tk(BT[r, j, :], c),
                              start=True, stop=True)
                last.then_inc(S("l_ps"), 1)
                for cp, hp, ci, j in pairs:
                    r, q, c = slice(64 * hp, 64 * hp + 64), slice(64 * cp, 64 * cp + 64), 2 * ci + cp
                    last = mm(ps[q, 2 + 2 * hp + ci, 128 * j:128 * j + 128], tk(BT[r, j, :], c),
                              AR[r, j, :, 64 * c:64 * c + 64], start=True, stop=True)
                last.then_inc(S("lt_ps"), 1)
                gate_half()
                pe.wait_ge(S("x0_done"), hh + 1)
                pe.wait_ge(S("lt_done"), hh + 1)
                for cp, hp, ci, j in pairs:
                    r, q, c = slice(64 * hp, 64 * hp + 64), slice(64 * cp, 64 * cp + 64), 2 * ci + cp
                    last = mm(ps[q, 2 * hp + ci, 128 * j:128 * j + 128], tk(KTT[r, j, :], c),
                              AR[r, j, :, 64 * c:64 * c + 64], start=True, stop=True)
                last.then_inc(S("mt_ps"), 1)
                for ci in range(2):
                    for j in range(HJ):
                        last = tp(ps[:, 4 + ci, 128 * j:128 * j + 128], AR[:, j, 0, 128 * ci:128 * ci + 128])
                last.then_inc(S("at_ps"), 1)
                pe.wait_ge(S("mt_done"), hh + 1)
                for ci in range(2):
                    for j in range(HJ):
                        last = tp(ps[:, ci, 128 * j:128 * j + 128], BT[:, j, 128 * ci:128 * ci + 128])
                last.then_inc(S("bt_ps"), 1)
                for cp, hp, ci, j in pairs:
                    q = slice(64 * cp, 64 * cp + 64)
                    last = mm(ps[q, 2 + hp, 256 * ci + 64 * j:256 * ci + 64 * j + 64], blk(U(10), hp, ci, j)[q],
                              blk(U(7), hp, ci, j)[q], start=True, stop=True)
                last.then_inc(S("mv_ps"), 1)
                pe.wait_ge(S("at_done"), hh + 1)
                for ci in range(2):
                    for j in range(HJ):
                        last = tp(ps[:, 4 + ci, 128 * j:128 * j + 128], KTT[:, j, 128 * ci:128 * ci + 128])
                last.then_inc(S("kt_ps"), 1)
                pe.wait_ge(S("bt_done"), hh + 1)
                for lv in range(1, 6):
                    pe.wait_ge(S("ltm_done"), 5 * hh + lv)
                    for hp in range(2):
                        pe.wait_ge(S("x_done"), 10 * hh + 2 * (lv - 1) + hp + 1)
                        for cp, ci, j in quads:
                            q = slice(64 * cp, 64 * cp + 64)
                            last = mm(ps[q, hp, 256 * ci + 64 * j:256 * ci + 64 * j + 64], blk(U(6), hp, ci, j)[q],
                                      blk(U(12), hp, ci, j)[q], start=True, stop=True)
                        last.then_inc(S("v1_ps"), 1)
                    if lv in (2, 4):
                        gate_half()
                    if lv == 1:
                        pe.wait_ge(S("mv_done"), hh + 1)
                        pe.wait_ge(S("kt_done"), hh + 1)
                    for w, ev in ((0, "w_ps"), (1, "wt_ps"))[lv == 5:]:
                        for hp in range(2):
                            if not w or lv == 5:
                                pe.wait_ge(S("v1_done"), 10 * hh + 2 * (lv - 1) + hp + 1)
                            pe.wait_ge(S("xt_done"), 12 * hh + 2 * (lv - 1) + hp + 1)
                            for cp, ci, j in quads:
                                q = slice(64 * cp, 64 * cp + 64)
                                o = slice(256 * ci + 64 * j, 256 * ci + 64 * j + 64)
                                v1, xt = blk(U(14), hp, ci, j)[q], blk(U(13), hp, ci, j)[q]
                                if w:
                                    last = mm(ps[q, 4 + hp, o], v1, xt, start=True, stop=True)
                                else:
                                    last = mm(ps[q, 2 + hp, o], xt, v1, start=True, stop=True)
                            last.then_inc(S(ev), 1)
                pe.wait_ge(S("xt_done"), 12 * hh + 12)
                for cp, hp, ci, j in pairs:
                    q = slice(64 * cp, 64 * cp + 64)
                    last = mm(ps[q, 2 + 2 * hp + ci, 128 * j:128 * j + 128], blk(U(13), hp, ci, j)[q],
                              blk(MVA, hp, ci, j, 128)[q], start=True, stop=True)
                last.then_inc(S("ua_ps"), 1)
                pe.wait_ge(S("ua_done"), hh + 1)

                def nU(hp, ci, j):
                    return blk(UA, hp, ci, j, 128)[:, 0:64]

                def nA(hp, ci, j):
                    return blk(UA, hp, ci, j, 128)[:, 64:128]

                for cp, hp, ci, j in pairs:
                    q, r, o = slice(64 * cp, 64 * cp + 64), slice(64 * hp, 64 * hp + 64), slice(256 * ci + 64 * j, 256 * ci + 64 * j + 64)
                    last = mm(ps[r, cp, o], nA(hp, ci, j)[q], blk(U(9), hp, ci, j)[q], start=True, stop=True)
                last.then_inc(S("rb_ps"), 1)
                for cp, hp, ci, j in pairs:
                    q, r, o = slice(64 * cp, 64 * cp + 64), slice(64 * hp, 64 * hp + 64), slice(256 * ci + 64 * j, 256 * ci + 64 * j + 64)
                    last = mm(ps[r, 2 + cp, o], nA(hp, ci, j)[q], blk(U(2), hp, ci, j)[q], start=True, stop=True)
                last.then_inc(S("g_ps"), 1)
                for cp, hp, ci, j in pairs:
                    q, r, o = slice(64 * cp, 64 * cp + 64), slice(64 * hp, 64 * hp + 64), slice(256 * ci + 64 * j, 256 * ci + 64 * j + 64)
                    mm(ps[r, 4 + cp, o], blk(U(3), hp, ci, j)[q], blk(U(7), hp, ci, j)[q], start=True, stop=False)
                    last = mm(ps[r, 4 + cp, o], blk(U(2), hp, ci, j)[q], nU(hp, ci, j)[q], start=False, stop=True)
                last.then_inc(S("f_ps"), 1)
                gate_half()
                pe.wait_ge(S("rb_done"), hh + 1)
                for cp, hp, ci, j in pairs:
                    q, o = slice(64 * cp, 64 * cp + 64), slice(256 * ci + 64 * j, 256 * ci + 64 * j + 64)
                    mm(ps[q, hp, o], blk(U(11), hp, ci, j)[q], blk(U(7), hp, ci, j)[q], start=True, stop=False)
                    last = mm(ps[q, hp, o], blk(U(9), hp, ci, j)[q], nU(hp, ci, j)[q], start=False, stop=True)
                last.then_inc(S("y0_ps"), 1)
                pe.wait_ge(S("g_done"), hh + 1)
                pe.wait_ge(S("f_done"), hh + 1)

                def state(c, hp, j):
                    s = U(14)[:, 0:256] if c == 1 else U(6)[:, 256 * (c - 2):256 * (c - 2) + 256]
                    return s[64 * hp:64 * hp + 64, 64 * j:64 * j + 64]

                for c in (1, 2):
                    ci, cp = divmod(c, 2)
                    if c > 1:
                        pe.wait_ge(S("s_done"), 2 * hh + c - 1)
                    for j in range(HJ):
                        for hp in range(2):
                            r = slice(64 * hp, 64 * hp + 64)
                            o = 512 * cp + 256 * ci + 64 * j
                            last = mm(ps[r, 6, 256 * (c - 1) + 64 * j:256 * (c - 1) + 64 * j + 64], U(10)[r, o:o + 64], state(c, hp, j),
                                      start=True, stop=True)
                    last.then_inc(S("s_ps"), 1)
                    if c == 1:
                        gate_half()
                pe.wait_ge(S("s_done"), 2 * hh + 2)
                for c in (1, 2, 3):
                    ci, cp = divmod(c, 2)
                    for j in range(HJ):
                        for hp in range(2):
                            r = slice(64 * hp, 64 * hp + 64)
                            last = mm(ps[64 * cp:64 * cp + 64, 2 + hp, 256 * ci + 64 * j:256 * ci + 64 * j + 64],
                                      tk(AR[r, j, 1, :], c), state(c, hp, j), start=True, stop=True)
                last.then_inc(S("yy_ps"), 1)
                gate_half()
                gate_half()
                pe.wait_ge(S("y0_done"), hh + 1)
                for j in range(HJ):
                    o = ps[:, 4 + j // 2, 256 * (j % 2):256 * (j % 2) + 256]
                    mm(o, g1w[:, hc + 128 * j:hc + 128 * j + 128], lz[:, 1, :], start=True, stop=False)
                    last = mm(o, g2w[0:32, hc + 128 * j:hc + 128 * j + 128], lz[0:32, 2, :], start=False, stop=True)
                last.then_inc(S("gt_ps"), 1)
                pe.wait_ge(S("yn_done"), hh + 1)
                for j in range(HJ):
                    for ci in range(2):
                        last = tp(ps[:, j // 2, 256 * (j % 2) + 128 * ci:256 * (j % 2) + 128 * ci + 128],
                                  U(4)[:, 512 * ci + 128 * j:512 * ci + 128 * j + 128])
                last.then_inc(S("ynt_ps"), 1)

            assert gate_part[0] == 32
            pe.wait_ge(S("y_done"), HALVES)
            with pe.Fori(0, 2) as i:
                for b in range(2):
                    for g in range(2):
                        n = NM + 2 * b + g
                        full(n, i, 4)
                        pe.wait_ge(S(("m1_done", "m2_done")[g]), i * 2 + (b + 1))
                        for t in range(TT):
                            for k in range(8):
                                last = mm(ps[:, 2 * g + t, :], (attnT, yT)[g][:, k, 128 * t:128 * t + 128],
                                          slot(n)[:, k, :], start=k == 0, stop=k == 7)
                        last.then_inc(S("chunk_used"), 1)
            pe.wait_ge(S("mg_done"), 4)
            transposes(mg, "mtr_ps")
            pe.wait_ge(S("mtr_done"), 8)
            for c in range(8):
                nb, h = divmod(c, 2)
                full(NO + c)
                for t in range(TT):
                    for k in range(8):
                        last = mm(ps[:, 2 * nb + t, :], mT[:, 8 * h + k, 128 * t:128 * t + 128], slot(NO + c)[:, k, :],
                                  start=h == 0 and k == 0, stop=h == 1 and k == 7)
                last.then_inc(S("chunk_used"), 1)

            pe.wait_ge(S("hfn_done"), 2)
            transposes(hfn, "ft_ps")
            pe.wait_ge(S("hft_done"), 8)
            pe.wait_ge(S("rw_in"), 32)
            for t in range(TT):
                for k in range(KT):
                    last = mm(ps[:, t, 0:36], hfT[:, k, 128 * t:128 * t + 128], rw[:, k, :], start=k == 0, stop=k == KT - 1)
            last.then_inc(S("lg_ps"), 1)
            pe.wait_ge(S("picks"), 1)
            AM = rs[:, 0:64].rearrange("p (a e) -> p a e", a=TT)
            mm(ps[:, 2, 0:32], C("upper"), AM[:, 0, :], start=True, stop=True)
            mm(ps[:, 3, 0:32], C("upper"), AM[:, 1, :], start=True, stop=False)
            mm(ps[:, 3, 0:32], C("ones"), AM[:, 0, :], start=False, stop=True)
            mm(ps[:, 4, 0:32], C("ones"), AM[:, 0, :], start=True, stop=False)
            mm(ps[:, 4, 0:32], C("ones"), AM[:, 1, :], start=False, stop=True).then_inc(S("pos_ps"), 1)
            pe.wait_ge(S("flag_set"), 1)

            def gather(q, b_free):
                pe.wait_ge(S(f"b{q % 2}_free"), b_free)
                for k in range(4):
                    for t in range(TT):
                        last = mm(ps[:, 6 + q % 2, 128 * k:128 * k + 128],
                                  hfn[:, t, 512 * q + 128 * k:512 * q + 128 * k + 128], OH[:, 128 * t:128 * t + 128],
                                  start=t == 0, stop=t == 1)
                last.then_inc(S(f"b{q % 2}_full"), 1)

            pe.wait_ge(S("oh_done"), 1)
            for q in range(4):
                gather(q, q // 2 + 1)
            with pe.Fori(0, GROUPS) as g:
                pe.wait_ge(S("b0_free"), g * 7 + 3)
                pe.wait_ge(S("b1_free"), g * 7 + 3)
                pe.wait_ge(S("hid_done"), g + 1)
                for c in range(16):
                    n = NE + c
                    full(n, g, PER_G)
                    w = ring[:, n % RING, :].rearrange("p (j k h) -> p j k h", j=GE, k=2)
                    for kk in range(2):
                        k = 2 * (c // 2) + kk
                        for j in range(GE):
                            last = mm(ps[32 * j:32 * j + 32, c % 2, :], XS[:, k, 32 * j:32 * j + 32], w[:, j, kk, :],
                                      start=k == 0, stop=k == KT - 1, tile_position=(0, 32 * j))
                    last.then_inc(S("chunk_used"), 1)
                    if c == 3:
                        for t in range(TT):
                            last = tp(ps[:, 6, 128 * t:128 * t + 128], OHW[:, 128 * t:128 * t + 128])
                        last.then_inc(S("b0_full"), 1)
                pe.wait_ge(S("hid_done"), g + 2)
                for k in range(4):
                    last = tp(ps[:, 7, 128 * k:128 * k + 128], HIDB[:, 128 * k:128 * k + 128])
                last.then_inc(S("b1_full"), 1)
                pe.wait_ge(S("b1_free"), g * 7 + 4)
                pe.wait_ge(S("ys_done"), g + 1)
                for c in range(8):
                    n = NE + 16 + c
                    kh, nh = divmod(c, 2)
                    full(n, g, PER_G)
                    w = ring[:, n % RING, :].rearrange("p (j n) -> p j n", j=GE)
                    for nb in range(2):
                        for j in range(GE):
                            last = mm(ps[32 * j:32 * j + 32, 2 + 2 * nh + nb, :], HIDT[:, kh, 32 * j:32 * j + 32],
                                      w[:, j, 512 * nb:512 * nb + 512], start=kh == 0, stop=kh == 3,
                                      tile_position=(0, 32 * j))
                    last.then_inc(S("chunk_used"), 1)
                    if c == 1:
                        pe.wait_ge(S("oh_done"), g + 2)
                    if 1 <= c < 5:
                        gather(c - 1, g * 7 + (4 + (c - 1) // 2))
                pe.wait_ge(S("ys_done"), g + 2)
                for u in range(8):
                    t, nb = divmod(u, 4)
                    pe.wait_ge(S(f"b{u % 2}_free"), g * 7 + (6 + u // 2))
                    mm(ps[:, 6 + u % 2, :], CTB[:, 128 * t:128 * t + 128], YS[:, 512 * nb:512 * nb + 512],
                       start=True, stop=True).then_inc(S(f"b{u % 2}_full"), 1)

            over = pe.value_load(flag[0:1, 0:1], min_val=0, max_val=1)
            with pe.If(over > 0):
                pe.wait_ge(S("b0_free"), 7 * GROUPS + 3)
                pe.wait_ge(S("b1_free"), 7 * GROUPS + 3)
                pe.sem_inc(S("fb_dn_ps"), 1)
                with pe.Fori(0, NEXP) as e:
                    pe.wait_ge(S("fb_up_in"), e * 64 + 64)
                    pe.wait_ge(S("fb_acc"), e * 2 + 1)
                    for w in range(2):
                        for t in range(TT):
                            for k in range(KT):
                                last = mm(ps[:, 2 * w + t, :], hfT[:, k, 128 * t:128 * t + 128],
                                          slot(2 * w + k // 8)[:, k % 8, :], start=k == 0, stop=k == KT - 1)
                    last.then_inc(S("fb_up_used"), 1)
                    pe.wait_ge(S("fb_hid"), e + 1)
                    for t in range(TT):
                        for k in range(4):
                            last = tp(ps[:, 4 + t, 128 * k:128 * k + 128], fHID[:, 512 * t + 128 * k:512 * t + 128 * k + 128])
                    last.then_inc(S("fb_ht_ps"), 1)
                    pe.wait_ge(S("fb_ht"), e + 1)
                    pe.wait_ge(S("fb_down_in"), e * 32 + 32)
                    for t in range(TT):
                        for nb in range(4):
                            for k in range(4):
                                last = mm(ps[:, 4 * t + nb, :], fHT[:, 512 * t + 128 * k:512 * t + 128 * k + 128],
                                          ring[:, k // 2, 2048 * (k % 2) + 512 * nb:2048 * (k % 2) + 512 * nb + 512],
                                          start=k == 0, stop=k == 3)
                        last.then_inc(S("fb_dn_ps"), 1)
                pe.nop()

        @block.scalar
        def _(act):
            f = nc.scalar.activation
            own = Steps(S("act_step"))
            xv = a["x"][0].rearrange("(a p) d -> p a d", p=P)
            for t in range(TT):
                act.dma_start(x_sb[:, t, :], xv[:, t, :]).then_inc(S(f"x_in{t}"), 16)
            act.dma_start(cst[:, :], a["consts"]).then_inc(S("const_in"), 16)
            act.wait_ge(S("vrow_zero"), 1)

            def rows(name, src, at=0, n=None):
                r = VEC[name] + at
                act.dma_start(vrow[r:r + n, 0:src.shape[-1]], src).then_inc(S("vec_in"), 16)

            rows("anorm", a["attn_norm_w"][0].rearrange("(k p) -> k p", p=P), n=16)
            act.dma_start(fnorm[:, :], a["ffn_norm_w"][0].rearrange("(p k) -> p k", p=P)).then_inc(S("vec_in"), 16)
            mixw = a["shift_mix"]
            rows("mix", mixw[0, 3 * RW:3 * RW + 256].rearrange("(k p) -> k p", p=P), n=2)
            rows("mix", mixw[0:1, 3 * RW + 256:3 * RW + 288], at=2, n=1)
            rows("mix", mixw[0, 0:3 * RW].rearrange("(k p) -> k p", p=P), at=3, n=24)
            for name, key in (("k_k", "rwkv_k_k"), ("k_a", "rwkv_k_a"), ("a0", "rwkv_a0"), ("ln_w", "rwkv_ln_w"),
                              ("ln_b", "rwkv_ln_b")):
                rows(name, a[key][0].rearrange("(k p) -> k p", p=P), n=8)
            act.dma_start(vrow[VEC["r_k"]:VEC["r_k"] + 8, :], a["rwkv_r_k"][0].rearrange("(k h) d -> k (h d)", h=2))\
                .then_inc(S("vec_in"), 16)
            act.dma_start(sink[:, :], a["attn_sinks"][0].partition_broadcast(P)).then_inc(S("small_in"), 16)
            act.dma_start(wua[0:64, :], a["rwkv_w_up"][0]).then_inc(S("small_in"), 16)
            act.dma_start(wua[64:128, :], a["rwkv_a_up"][0]).then_inc(S("small_in"), 16)
            act.dma_start(g1w[:, :], a["rwkv_g_up"][0, 0:128, :]).then_inc(S("small_in"), 16)
            act.dma_start(g2w[0:32, :], a["rwkv_g_up"][0, 128:160, :]).then_inc(S("small_in"), 16)
            act.dma_start(w0row[0:1, :], a["rwkv_w0"]).then_inc(S("small_in"), 16)
            act.dma_start(rbias[:, 0:4], a["router_group_b"][0].partition_broadcast(P)).then_inc(S("small_in"), 16)
            act.dma_start(rbias[:, 4:36], a["router_expert_b"][0].partition_broadcast(P)).then_inc(S("rb_in"), 16)

            def squares(src, dst, ev):
                for t in range(TT):
                    f(dst[:, t, :], src[:, t, :], ACT.Square, accum_out=rstd[:, t:t + 1]).then_inc(S(ev), 1)

            for t in range(TT):
                act.wait_ge(S(f"x_in{t}"), 16)
            squares(x_sb, junk, "ss_done")
            act.wait_ge(S("ms_done"), 1)
            f(rstd[:, 2:4], rstd[:, 2:4], ACT.Sqrt).then_inc(S("rt_done"), 1)

            act.wait_ge(S("vt_done"), 1)
            act.wait_ge(S("ht_done"), 8)
            f(h_hi[:, :, :], hT, ACT.Copy).then_inc(S("h_hi_done"), 1)
            for t, m in enumerate((128, 128, 32)):
                act.wait_ge(*((S("z_ps"), t + 1) if t < 2 else (S("chunk_used"), NZ)))
                f(lz[0:m, t, :], ps[0:m, 4 + t, 0:TOK], ACT.Copy, scale=omm[0:m, t:t + 1]).then_inc(S("za_done"), 1)
            with act.Fori(0, 3) as i:
                def z_out(e):
                    c = 4 * (e // 8) + e % 4
                    act.wait_ge(S("w_used"), i * 16 + (4 + e + 1))
                    f(zT[:, bass.ds(i * 8 + c, 1), :].rearrange("p a t -> p (a t)"), ps[:, c, 0:TOK], ACT.Copy,
                      scale=omm[:, bass.ds(i * 8 + 3 + c, 1)]).then_inc(S("za_done"), 1)

                for x in range(16):
                    n, src = z_piece(x)
                    if x % 4 == 0:
                        act.wait_ge(S(f"slot_full{n % RING}"), i * 16 + 16 * (n // RING + 1))
                    act.wait_ge(S("w_used"), i * 16 + (x + 1))
                    f(pieces(x % 4)[0].rearrange("p (k n) -> p k n", k=8), src, ACT.Copy).then_inc(S("w_hi"), 1)
                    if (x - LAG) % 8 >= 4 and x >= LAG:
                        z_out(x - LAG)
                for e in range(16 - LAG, 16):
                    z_out(e)
            act.wait_ge(S("z_done"), 3)
            f(lz[0:64, 0, :], lz[0:64, 0, :], ACT.Tanh).then_inc(S("lora_done"), 1)
            f(lz[:, 1, :], lz[:, 1, :], ACT.Sigmoid).then_inc(S("lora_done"), 1)
            f(lz[0:32, 2, :], lz[0:32, 2, :], ACT.Sigmoid).then_inc(S("lora_done"), 1)

            def qkv_out(e):
                c = 4 * (e // 8) + e % 4
                act.wait_ge(S("w_used"), 4 + UZ + (e if c < 10 else UQ - 1) + 1)
                if c < 8:
                    f(qT[:, c, :], ps[:, c, 0:TOK], ACT.Copy, scale=HD ** -0.5).then_inc(S("qkv_done"), 1)
                elif c < 10:
                    f(kTa[:, c - 8, :], ps[:, c - 8, 0:TOK], ACT.Copy).then_inc(S("qkv_done"), 1)
                else:
                    f(vA[:, c - 10, :], ps[:, c - 8, 0:KV_W], ACT.Copy).then_inc(S("qkv_done"), 1)

            for x in range(UQ + LAG):
                if x < UQ:
                    n, src, shape = q_piece(x)
                    if x % 4 == 0:
                        act.wait_ge(S(f"slot_full{n % RING}"), 16 * (n // RING + 1))
                    buf, used = q_buffer(x)
                    act.wait_ge(S("w_used"), used)
                    f(shape(pieces(buf)[0]), src, ACT.Copy).then_inc(S("w_hi"), 1)
                if x >= LAG and (x - LAG) % 8 >= 4:
                    qkv_out(x - LAG)

            gate_tile = [0]

            def gate_out():
                q = gate_tile[0]
                gate_tile[0] += 1
                b, t = divmod(q, 2)
                act.wait_ge(*((S("chunk_used"), NG + 2 * b + 2) if t else (S("gate_ps"), b + 1)))
                if q >= 2:
                    act.wait_ge(S(f"gate_stored{t}"), 16 * b)
                f(gtmp[:, t, :], ps[:, 7, :], ACT.Sigmoid).then_inc(S("gate_out"), 1)
                act.wait_ge(S("gate_out"), q + 1)
                act.dma_start(gate_d[:, t, 512 * b:512 * b + 512], gtmp[:, t, :]).then_inc(S(f"gate_stored{t}"), 16)

            for u in range(4):
                n, hg = divmod(u, 2)
                w = 128 * (n + 1)
                act.wait_ge(S("sm_done"), u + 1)
                f(probs[:, :, 0:w], probs[:, :, 0:w], ACT.Exp).then_inc(S("ex_done"), 1)
                f(aes[:, :], aes[:, :], ACT.Exp).then_inc(S("ex_done"), 1)
                act.wait_ge(S("pt_ps"), u + 1)
                for kb in range(n + 1):
                    f(probsT[:, kb, :, :], ps[:, 4 - 2 * kb:6 - 2 * kb, :].rearrange("p b (h q) -> p (b h) q", h=4),
                      ACT.Copy).then_inc(S("pt_done"), 1)
                act.wait_ge(S("pv_ps"), u + 1)
                f(attnT[:, 4 * hg:4 * hg + 4, 128 * n:128 * n + 128], ps[:, 0, :].rearrange("p (c q) -> p c q", c=4),
                  ACT.Copy).then_inc(S("pv_done"), 1)
                gate_out()

            for hh in range(HALVES):
                act.wait_ge(S("wl_ps"), hh + 1)
                f(U(4).rearrange("p (b n) -> p b n", b=2), ps[:, 0:2, :], ACT.Sigmoid).then_inc(S("sg_done"), 1)
                act.wait_ge(S("a_ps"), hh + 1)
                for j in range(HJ):
                    last = f(U(5)[:, 256 * j:256 * j + 256], ps[:, 2 + j // 2, 256 * (j % 2):256 * (j % 2) + 256],
                             ACT.Sigmoid, bias=vec("a0", HJ * hh + j))
                last.then_inc(S("a_done"), 1)
                act.wait_ge(S("kkr_done"), hh + 1)
                f(U(7), U(6), ACT.Square).then_inc(S("sq_done"), 1)
                act.wait_ge(S("cum_ps"), hh + 1)
                for bk, g0, gn_ in ((4, 0, 6), (0, 6, 2)):
                    cum = ps[:, bk:bk + gn_ // 2, :].rearrange("p b (t w n) -> p (b t) w n", t=2, w=2)
                    for dst, w, sgn in ((8, 0, 1.0), (9, 0, -1.0), (10, 1, 1.0)):
                        last = f(U(dst).rearrange("p (g n) -> p g n", g=8)[:, g0:g0 + gn_, :], cum[:, :, w, :], ACT.Exp,
                                 scale=sgn * DECAY_C)
                last.then_inc(S("P_done"), 1)
                act.wait_ge(S("ks_ps"), hh + 1)
                f(U(11).rearrange("p (b n) -> p b n", b=2), ps[:, 1:3, :], ACT.Sqrt).then_inc(S("nrm_done"), 1)

                gate_out()

                def byhead(dst, banks, ev):
                    f(dst, ps[:, banks:banks + 2, :].rearrange("p b (j h x) -> p (b j) h x", j=4, h=2), ACT.Copy)\
                        .then_inc(S(ev), 1)

                def blocks(ap, w):
                    return ap.rearrange("p (h g x) -> p g h x", h=2, g=8, x=w)

                act.wait_ge(S("vtr_ps"), hh + 1)
                byhead(blocks(U(7), 64), 2, "vt2_done")
                gate_out()
                gate_out()
                act.wait_ge(S("at_ps"), hh + 1)
                byhead(blocks(U(4, 2), 128)[:, :, :, 64:128], 4, "at_done")
                act.wait_ge(S("bt_ps"), hh + 1)
                byhead(blocks(U(2), 64), 0, "bt_done")
                act.wait_ge(S("kt_ps"), hh + 1)
                byhead(blocks(U(3), 64), 4, "kt_done")
                act.wait_ge(S("mv_ps"), hh + 1)
                f(U(4, 2).rearrange("p (g x) -> p g x", g=16)[:, :, 0:64],
                  ps[:, 2:4, :].rearrange("p b (g x) -> p (b g) x", g=8), ACT.Copy).then_inc(S("mv_done"), 1)
                for lv in range(1, 6):
                    for hp in range(2):
                        act.wait_ge(S("v1_ps"), 10 * hh + 2 * (lv - 1) + hp + 1)
                        if lv > 1:
                            act.wait_ge(S("wt_ps"), 10 * hh + 2 * (lv - 2) + hp + 1)
                        f(U(14)[:, 512 * hp:512 * hp + 512], ps[:, hp, :], ACT.Copy).then_inc(S("v1_done"), 1)
                    if lv == 4:
                        gate_out()
                act.wait_ge(S("ua_ps"), hh + 1)
                f(U(12, 2).rearrange("p (b n) -> p b n", b=4), ps[:, 2:6, :], ACT.Copy, scale=-1.0)\
                    .then_inc(S("ua_done"), 1)
                act.wait_ge(S("y0_ps"), hh + 1)
                f(U(8).rearrange("p (b n) -> p b n", b=2), ps[:, 0:2, :], ACT.Copy).then_inc(S("y0_done"), 1)
                gate_out()
                act.wait_ge(S("yc_done"), hh + 1)
                f(U(4), U(5), ACT.Square).then_inc(S("ysq_done"), 1)
                act.wait_ge(S("var_done"), hh + 1)
                f(gn[:, 1, :], gn[:, 1, :], ACT.Sqrt).then_inc(S("gsd_done"), 1)
                gate_out()

            act.wait_ge(S("y_done"), HALVES)
            act.dma_start(x_sb[:, :, :], xv).then_inc(S("x2_in"), 16)
            act.dma_start(rw[:, :, 0:4], a["router_group_w"][0].rearrange("(p k) n -> p k n", p=P)).then_inc(S("rw_in"), 16)
            act.dma_start(rw[:, :, 4:36], a["router_expert_w"][0].rearrange("(p k) n -> p k n", p=P)).then_inc(S("rw_in"), 16)
            assert gate_tile[0] == 16
            act.wait_ge(S("gate_stored0"), 16 * 8)
            act.wait_ge(S("gate_stored1"), 16 * 8)
            for nb in range(4):
                if nb >= 2:
                    act.wait_ge(S("mg_done"), nb - 1)
                for g in range(2):
                    act.dma_start(gates[nb % 2][g], gate_d[:, :, D * g + 512 * nb:D * g + 512 * nb + 512])\
                        .then_inc(S(f"gate_in{nb % 2}"), 16)
            act.wait_ge(S("mg_done"), 4)
            act.dma_start(FW, a["final_norm_w"].partition_broadcast(P)).then_inc(S("fw_in"), 16)
            act.wait_ge(S("x2_done"), 4)
            squares(x_sb, junk2, "ss_done")
            act.wait_ge(S("ms_done"), 2)
            f(rstd[:, 2:4], rstd[:, 2:4], ACT.Sqrt).then_inc(S("rt_done"), 1)
            act.wait_ge(S("rt_in"), 1)
            f(rs[:, 400:408], rs[:, 400:408], ACT.Exp).then_inc(S("rt_ex"), 1)
            act.wait_ge(S("rt_in"), 2)
            f(rs[:, 408:410], rs[:, 408:410], ACT.Exp).then_inc(S("rt_ex"), 1)
            act.sem_inc(S("ys_done"), 1)
            with act.Fori(0, GROUPS) as g:
                act.wait_ge(S("b0_full"), g * 7 + 3)
                f(CTB, ps[:, 6, 0:256], ACT.Copy).then_inc(S("b0_free"), 1)
                act.wait_ge(S("chunk_used"), g * PER_G + (NE + 16))
                f(SG, ps[:, 0, :], ACT.Sigmoid).then_inc(S("sgh_done"), 1)
                act.wait_ge(S("b1_full"), g * 7 + 3)
                f(HIDT.rearrange("p k s -> p (k s)"), ps[:, 7, :], ACT.Copy).then_inc(S("b1_free"), 1)
                act.wait_ge(S("chunk_used"), g * PER_G + (NE + PER_G))
                f(YS.rearrange("p (b n) -> p b n", b=4), ps[:, 2:6, :], ACT.Copy).then_inc(S("ys_done"), 1)
            act.wait_ge(S("b0_free"), 7 * GROUPS + 3)
            act.wait_ge(S("b1_free"), 7 * GROUPS + 3)
            over = act.value_load(flag[0:1, 0:1], min_val=0, max_val=1)
            with act.If(over > 0):
                with act.Fori(0, NEXP) as e:
                    act.wait_ge(S("fb_up_used"), e + 1)
                    f(fSG.rearrange("p (b n) -> p b n", b=2), ps[:, 0:2, :], ACT.Sigmoid).then_inc(S("fb_sg"), 1)
                    act.wait_ge(S("fb_ht_ps"), e + 1)
                    f(fHT.rearrange("p (b n) -> p b n", b=2), ps[:, 4:6, :], ACT.Copy).then_inc(S("fb_ht"), 1)
                act.wait_ge(S("fb_acc"), TT * NEXP + 1)
                act.nop()
            squares(x_sb, junk2, "ss_done")
            act.wait_ge(S("ms_done"), 3)
            f(rstd[:, 2:4], rstd[:, 2:4], ACT.Sqrt).then_inc(S("rt_done"), 1)

        @block.vector
        def _(dve):
            v = nc.vector
            st = Steps(S("dve_step"))

            def step(ins):
                st.on(ins)
                st.last(dve)

            def inv_rms(r):
                dve.wait_ge(S("ss_done"), 2 * r + 2)
                v.tensor_scalar(rstd[:, 2:4], rstd[:, 0:2], 1.0 / D, NORM_EPS, ALU.mult, ALU.add).then_inc(S("ms_done"), 1)
                dve.wait_ge(S("rt_done"), r + 1)
                step(v.reciprocal(rstd[:, 4:6], rstd[:, 2:4]))

            def evac(dst, scale, ps_ev, ev):
                for g in range(8):
                    t, kq = divmod(g, 4)
                    dve.wait_ge(S(ps_ev), g + 1)
                    o = dst[:, 4 * kq:4 * kq + 4, 128 * t:128 * t + 128]
                    i = ps[:, g, :].rearrange("p (k t) -> p k t", k=4)
                    if scale:
                        v.tensor_tensor(o, i, rep(vec(scale, 4 * kq, 4), 128), ALU.mult).then_inc(S(ev), 1)
                    else:
                        v.tensor_copy(o, i).then_inc(S(ev), 1)

            inv_rms(0)
            for t in range(TT):
                v.tensor_scalar(xn[:, t, :], x_sb[:, t, :], rstd[:, 4 + t:5 + t], None, ALU.mult).then_inc(S("xn_done"), 1)
            dve.wait_ge(S("vt_ps"), 1)
            step(v.tensor_copy(vecT[:, 0:NVEC], ps[:, 0, 0:NVEC]))
            step(v.tensor_scalar(omm[:, :], vec("mix", 0, 27), -1.0, 1.0, ALU.mult, ALU.add))
            v.tensor_scalar(omka[:, :], vec("k_a", 0, 8), -1.0, 1.0, ALU.mult, ALU.add).then_inc(S("vt_done"), 1)
            dve.wait_ge(S("vt_done"), 1)
            evac(hT, "anorm", "xt_ps", "ht_done")
            dve.sem_inc(S("w_used"), 4)
            dve.wait_ge(S("h_hi_done"), 1)
            v.tensor_tensor(h_lo[:, :, :], hT, h_hi[:, :, :].bitcast(F32), ALU.subtract).then_inc(S("h_lo_done"), 1)

            for t, m in enumerate((128, 128, 32)):
                dve.wait_ge(S("za_done"), t + 1)
                v.scalar_tensor_tensor(out=lz[0:m, t, 1:TOK], in0=ps[0:m, 4 + t, 0:TOK - 1], scalar=vec("mix", t)[0:m],
                                       in1=lz[0:m, t, 1:TOK], op0=ALU.mult, op1=ALU.add).then_inc(S("z_done"), 1)
            with dve.Fori(0, 3) as i:
                def z_mix(e):
                    c = 4 * (e // 8) + e % 4
                    dve.wait_ge(S("za_done"), i * 8 + 4 + c)
                    z = zT[:, bass.ds(i * 8 + c, 1), 1:TOK].rearrange("p a t -> p (a t)")
                    v.scalar_tensor_tensor(out=z, in0=ps[:, c, 0:TOK - 1],
                                           scalar=vecT[:, bass.ds(i * 8 + (VEC["mix"] + 3 + c), 1)],
                                           in1=z, op0=ALU.mult, op1=ALU.add).then_inc(S("z_done"), 1)

                for x in range(16):
                    n, src = z_piece(x)
                    hi, lo = (o.rearrange("p (k n) -> p k n", k=8) for o in pieces(x % 4))
                    dve.wait_ge(S("w_hi"), i * 16 + (x + 1))
                    v.tensor_tensor(lo, src, hi.bitcast(F32), ALU.subtract).then_inc(S("w_lo"), 1)
                    if x % 4 == 3:
                        dve.wait_ge(S("w_lo"), i * 16 + (x + 1))
                        dve.sem_inc(S("chunk_used"), 1)
                    if (x - LAG) % 8 >= 4 and x >= LAG:
                        z_mix(x - LAG)
                for e in range(16 - LAG, 16):
                    z_mix(e)
            for x in range(UQ):
                n, src, shape = q_piece(x)
                hi, lo = (shape(o) for o in pieces(q_buffer(x)[0]))
                dve.wait_ge(S("w_hi"), UZ + x + 1)
                v.tensor_tensor(lo, src, hi.bitcast(F32), ALU.subtract).then_inc(S("w_lo"), 1)
                if x % 4 == 3:
                    dve.wait_ge(S("w_lo"), UZ + x + 1)
                    dve.sem_inc(S("chunk_used"), 1)
            dve.wait_ge(S("z_done"), 27)

            dve.wait_ge(S("small_in"), 16 * 7)
            for u in range(4):
                n, hg = divmod(u, 2)
                w = 128 * (n + 1)
                sc = ps[:, 0:4, :].rearrange("p b (j k) -> p (b j) k", j=2)
                dve.wait_ge(S("sc_ps"), u + 1)
                for h in range(8):
                    head = 8 * hg + h
                    slope = 2.0 ** (-8.0 * (head + 1) / QH)
                    last = v.scalar_tensor_tensor(out=probs[:, h, 0:w], in0=C("dist", w, 256 - w), scalar=-slope,
                                                  in1=sc[:, h, 0:w], op0=ALU.mult, op1=ALU.add)
                step(last)
                step(v.tensor_reduce(amax[:, :], probs[:, :, 0:w], AX.X, ALU.max))
                step(v.tensor_tensor(amax[:, :], amax[:, :], sink[:, 8 * hg:8 * hg + 8], ALU.max))
                step(v.tensor_tensor(aes[:, :], sink[:, 8 * hg:8 * hg + 8], amax[:, :], ALU.subtract))
                v.tensor_tensor(probs[:, :, 0:w], probs[:, :, 0:w], rep(amax[:, :], w), ALU.subtract)\
                    .then_inc(S("sm_done"), 1)
                dve.wait_ge(S("ex_done"), 2 * u + 2)
                step(v.tensor_reduce(asum[:, :], probs[:, :, 0:w], AX.X, ALU.add))
                step(v.tensor_tensor(asum[:, :], asum[:, :], aes[:, :], ALU.add))
                step(v.reciprocal(asum[:, :], asum[:, :]))
                v.tensor_tensor(probs[:, :, 0:w], probs[:, :, 0:w], rep(asum[:, :], w), ALU.mult)\
                    .then_inc(S("pr_done"), 1)
            dve.wait_ge(S("pv_ps"), 4)

            for hh in range(HALVES):
                def ch(ap):
                    return ap.rearrange("p (j t) -> p j t", j=HJ)

                def g16(ap):
                    return ap.rearrange("p (g x) -> p g x", g=16)

                c0 = HJ * hh
                zr, zk, zv = (zT[:, 8 * w + c0:8 * w + c0 + HJ, :] for w in range(3))
                AR = U(0, 2).rearrange("p (j w t) -> p j w t", j=HJ, w=2)
                if hh:
                    dve.wait_ge(S("y_done"), hh)
                v.tensor_tensor(ch(U(6)), zk, rep(vec("k_k", c0, HJ), TOK), ALU.mult).then_inc(S("kkr_done"), 1)
                dve.wait_ge(S("a_done"), hh + 1)
                for j in range(HJ):
                    last = v.tensor_scalar(ch(U(12))[:, j, :], ch(U(5))[:, j, :], vec("k_a", c0 + j),
                                           omka[:, c0 + j:c0 + j + 1], ALU.mult, ALU.add)
                step(last)
                dve.wait_ge(S("kkr_done"), hh + 1)
                step(v.tensor_tensor(zk, zk, ch(U(12)), ALU.mult))
                step(v.tensor_tensor(ch(U(12)), zr, zk, ALU.mult))
                v.tensor_tensor(ch(U(12)), ch(U(12)), rep(vec("r_k", c0, HJ), TOK), ALU.mult).then_inc(S("rk_done"), 1)
                dve.wait_ge(S("nrm_done"), hh + 1)
                step(v.tensor_scalar(U(11), U(11), 1e-12, None, ALU.max))
                step(v.reciprocal(U(11), U(11)))
                step(v.tensor_tensor(U(6), U(6), U(11), ALU.mult))
                dve.wait_ge(S("P_done"), hh + 1)
                v.tensor_tensor(AR[:, :, 0, :], ch(U(6)), ch(U(10)), ALU.mult)
                v.tensor_tensor(AR[:, :, 1, :], zr, ch(U(8)), ALU.mult)
                step(v.tensor_tensor(U(11), U(6), U(5), ALU.mult))
                v.tensor_tensor(U(2), U(11), U(9), ALU.mult)
                v.tensor_copy(pend[:, :].rearrange("p (b a j) -> p b a j", b=2, a=2),
                              U(8).rearrange("p (j a b t) -> p b a j t", j=HJ, a=2, b=2)[:, :, :, :, 63])
                v.tensor_tensor(ch(U(3)), zk, ch(U(9)), ALU.mult).then_inc(S("arbk"), 1)
                dve.wait_ge(S("arbk"), hh + 1)
                dve.wait_ge(S("bon_ps"), hh + 1)
                v.tensor_tensor(zr, ps[:, 4:6, :].rearrange("p b (j t) -> p (b j) t", j=2), zv, ALU.mult)\
                    .then_inc(S("bon_done"), 1)
                dve.wait_ge(S("l_ps"), hh + 1)
                v.tensor_tensor(g16(U(12)), ps[:, 0:2, :].rearrange("p b (g x) -> p (b g) x", g=8), tile16(C("m1L")),
                                ALU.mult).then_inc(S("x0_done"), 1)
                dve.wait_ge(S("x0_done"), hh + 1)
                v.scalar_tensor_tensor(out=g16(U(12)), in0=g16(U(12)), scalar=-1.0, in1=tile16(C("eye")),
                                       op0=ALU.mult, op1=ALU.add).then_inc(S("x_done"), 2)
                dve.wait_ge(S("lt_ps"), hh + 1)
                lt = ps[:, 2:6, :].rearrange("p b (g w x) -> p (b g) w x", g=4, w=2)
                v.tensor_tensor(g16(U(8)), lt[:, :, 0, :], tile16(C("mU")), ALU.mult)
                v.tensor_tensor(g16(U(9)), lt[:, :, 1, :], tile16(C("mUi")), ALU.mult).then_inc(S("lt_done"), 1)
                dve.wait_ge(S("lt_done"), hh + 1)
                step(v.tensor_tensor(g16(U(14)), g16(U(8)), tile16(C("lvlT", 64)), ALU.mult))
                v.scalar_tensor_tensor(out=g16(U(13)), in0=g16(U(14)), scalar=-1.0, in1=tile16(C("eye")),
                                       op0=ALU.mult, op1=ALU.add).then_inc(S("xt_done"), 2)
                dve.wait_ge(S("mt_ps"), hh + 1)
                mt = ps[:, 0:4, :].rearrange("p b (g w x) -> p (b g) w x", g=4, w=2)
                v.tensor_tensor(g16(U(10)), mt[:, :, 0, :], tile16(C("mU")), ALU.mult)
                v.tensor_tensor(g16(U(11)), mt[:, :, 1, :], tile16(C("mUi")), ALU.mult).then_inc(S("mt_done"), 1)
                for lv in range(1, 6):
                    for w, ev in ((0, "w_ps"), (1, "wt_ps"))[lv == 5:]:
                        for hp in range(2):
                            dve.wait_ge(S(ev), (8, 10)[w] * hh + 2 * (lv - 1) + hp + 1)
                            x = U(12 + w)[:, 512 * hp:512 * hp + 512]
                            if w:
                                dve.wait_ge(S("xt_done"), 12 * hh + 2 * (lv - 1) + hp + 1)
                            else:
                                dve.wait_ge(S("x_done"), 10 * hh + 2 * (lv - 1) + hp + 1)
                            v.tensor_tensor(x, x, ps[:, 2 + 2 * w + hp, :], ALU.subtract)\
                                .then_inc(S(("x_done", "xt_done")[w]), 1)
                dve.wait_ge(S("rb_ps"), hh + 1)
                for cp in range(2):
                    for ci in range(2):
                        rt = AR[:, :, 1, 128 * ci + 64 * cp:128 * ci + 64 * cp + 64]
                        last = v.tensor_tensor(rt, rt, ps[:, cp, 256 * ci:256 * ci + 256].rearrange(
                            "p (j x) -> p j x", j=HJ), ALU.add)
                last.then_inc(S("rb_done"), 1)
                dve.wait_ge(S("g_ps"), hh + 1)
                v.tensor_tensor(g16(U(10)), ps[:, 2:4, :].rearrange("p b (g x) -> p (b g) x", g=8), tile16(C("eye")),
                                ALU.add).then_inc(S("g_done"), 1)
                dve.wait_ge(S("f_ps"), hh + 1)
                v.tensor_tensor(g16(U(14)), ps[:, 4:6, :].rearrange("p b (g x) -> p (b g) x", g=8),
                                rep(pend[:, :], 64), ALU.mult).then_inc(S("f_done"), 1)
                dve.wait_ge(S("f_done"), hh + 1)
                for c in (1, 2):
                    ci, cp = divmod(c, 2)
                    o = 8 * cp + 4 * ci
                    s = U(6)[:, 256 * (c - 1):256 * c]
                    dve.wait_ge(S("s_ps"), 2 * hh + c)
                    step(v.tensor_tensor(s.rearrange("p (j x) -> p j x", j=HJ),
                                         ps[:, 6, 256 * (c - 1):256 * c].rearrange("p (j x) -> p j x", j=HJ),
                                         rep(pend[:, o:o + 4], 64), ALU.mult))
                    v.tensor_tensor(s, s, U(14)[:, 64 * o:64 * o + 256], ALU.add).then_inc(S("s_done"), 1)
                dve.wait_ge(S("yy_ps"), hh + 1)
                dve.wait_ge(S("y0_done"), hh + 1)
                Y = U(8)
                y2 = Y.rearrange("p (h n) -> p h n", h=2)
                step(v.tensor_tensor(y2[64:128], y2[64:128], ps[64:128, 2:4, :], ALU.add))
                step(v.tensor_tensor(y2[0:64, :, 256:512], y2[0:64, :, 256:512], ps[0:64, 2:4, 256:512], ALU.add))
                step(v.tensor_reduce(gn[:, 0, :], g16(Y), AX.X, ALU.add))
                step(v.tensor_scalar(gn[:, 0, :], gn[:, 0, :], 1.0 / HD, None, ALU.mult))
                v.tensor_tensor(g16(U(5)), g16(Y), rep(gn[:, 0, :], 64), ALU.subtract).then_inc(S("yc_done"), 1)
                dve.wait_ge(S("ysq_done"), hh + 1)
                step(v.tensor_reduce(gn[:, 1, :], g16(U(4)), AX.X, ALU.add))
                v.tensor_scalar(gn[:, 1, :], gn[:, 1, :], 1.0 / HD, GN_EPS, ALU.mult, ALU.add).then_inc(S("var_done"), 1)
                dve.wait_ge(S("gsd_done"), hh + 1)
                step(v.reciprocal(gn[:, 2, :], gn[:, 1, :]))
                for hp in range(2):
                    last = v.tensor_tensor(U(4).rearrange("p (g h x) -> p g h x", g=8, h=2)[:, :, hp, :],
                                           U(5)[:, 512 * hp:512 * hp + 512].rearrange("p (g x) -> p g x", g=8),
                                           rep(gn[:, 2, 8 * hp:8 * hp + 8], 64), ALU.mult)
                last.then_inc(S("yn_done"), 1)
                dve.wait_ge(S("ynt_ps"), hh + 1)
                for j in range(HJ):
                    last = v.tensor_scalar(ch(U(5))[:, j, :], ps[:, j // 2, 256 * (j % 2):256 * (j % 2) + 256],
                                           vec("ln_w", c0 + j), vec("ln_b", c0 + j), ALU.mult, ALU.add)
                step(last)
                dve.wait_ge(S("bon_done"), hh + 1)
                step(v.tensor_tensor(ch(U(5)), ch(U(5)), zr, ALU.add))
                dve.wait_ge(S("gt_ps"), hh + 1)
                v.tensor_tensor(zv, ch(U(5)), ps[:, 4:6, :].rearrange("p b (j t) -> p (b j) t", j=2), ALU.mult)\
                    .then_inc(S("y_done"), 1)

            dve.sem_inc(S("m1_done"), 1)
            dve.sem_inc(S("m2_done"), 1)
            with dve.Fori(0, 2) as i:
                for b in range(2):
                    ga, gb = gates[b]
                    dve.wait_ge(S(f"gate_in{b}"), i * 32 + 32)
                    for g in range(2):
                        dve.wait_ge(S("chunk_used"), i * 4 + (NM + 2 * b + g + 1))
                        v.tensor_tensor(gates[b][g], gates[b][g], ps[:, 2 * g:2 * g + 2, :], ALU.mult)\
                            .then_inc(S(("m1_done", "m2_done")[g]), 1)
                    dve.wait_ge(S("m1_done"), i * 2 + (b + 2))
                    dve.wait_ge(S("m2_done"), i * 2 + (b + 2))
                    v.tensor_tensor(mg[:, :, bass.ds(i * 1024 + 512 * b, 512)], ga, gb, ALU.add)\
                        .then_inc(S("mg_done"), 1)
            evac(mT, None, "mtr_ps", "mtr_done")
            dve.wait_ge(S("x2_in"), 16)
            for nb in range(4):
                dve.wait_ge(S("chunk_used"), NO + 2 * nb + 2)
                xs = x_sb[:, :, 512 * nb:512 * nb + 512]
                v.tensor_tensor(xs, xs, ps[:, 2 * nb:2 * nb + 2, :], ALU.add).then_inc(S("x2_done"), 1)
            dve.wait_ge(S("x2_done"), 4)
            inv_rms(1)
            for t in range(TT):
                v.tensor_scalar(hfn[:, t, :].rearrange("q (k p) -> q k p", k=KT),
                                x_sb[:, t, :].rearrange("q (p k) -> q k p", k=KT), rstd[:, 4 + t:5 + t], None, ALU.mult).then_inc(S("hfn_done"), 1)
            evac(hfT, "fnorm", "ft_ps", "hft_done")

            def R(at, n, w=None):
                r = rs[:, at:at + TT * n]
                return r.rearrange("p (a n) -> p a n", a=TT)

            AM, WT, POS, WOV = R(0, 32), R(64, 32), R(128, 32), R(192, 32)
            LG, EL, EQ, OH1 = R(256, 36), R(416, 32), R(480, 32), R(544, 32)
            GX, EX = R(400, 4), rs[:, 408:410]
            GM, GI, GOH, GS = rs[:, 608:610], rs[:, 610:612], R(612, 4), rs[:, 620:622]
            M1, M2, MI, W1, W2 = (rs[:, 622 + 2 * i:624 + 2 * i] for i in range(5))
            CNT = rs[:, 640:641]
            TMP = R(648, 32)
            iota = C("iota")
            dve.wait_ge(S("lg_ps"), 1)
            dve.wait_ge(S("rb_in"), 16)

            def both(ap, n):
                return ap.unsqueeze(1).to_broadcast([P, TT, n])

            step(v.tensor_tensor(LG, ps[:, 0:2, 0:36], both(rbias[:, :], 36), ALU.add))
            gl = LG[:, :, 0:4]
            step(v.tensor_reduce(GM, gl, AX.X, ALU.max))
            v.tensor_tensor(GX, gl, rep(GM, 4), ALU.subtract).then_inc(S("rt_in"), 1)
            step(v.tensor_tensor(GOH, gl, rep(GM, 4), ALU.is_equal))
            step(v.scalar_tensor_tensor(out=GOH, in0=GOH, scalar=-64.0, in1=both(iota[:, 0:4], 4), op0=ALU.mult, op1=ALU.add))
            step(v.tensor_reduce(GI, GOH, AX.X, ALU.min))
            step(v.tensor_tensor(GOH, GOH, rep(GI, 4), ALU.is_equal))
            step(v.tensor_scalar(GOH, GOH, 1.0, BIG, ALU.subtract, ALU.mult))
            step(v.tensor_copy(EL, LG[:, :, 4:36]))
            el8 = rs[:, 416:480].rearrange("p (g e) -> p g e", g=8)
            step(v.tensor_tensor(el8, el8, rep(rs[:, 612:620], 8), ALU.add))

            def first_best(m, oh):
                step(v.tensor_reduce(m, EL, AX.X, ALU.max))
                step(v.tensor_tensor(oh, EL, rep(m, 32), ALU.is_equal))
                step(v.scalar_tensor_tensor(out=oh, in0=oh, scalar=-64.0, in1=both(iota, 32), op0=ALU.mult, op1=ALU.add))
                step(v.tensor_reduce(MI, oh, AX.X, ALU.min))
                step(v.tensor_tensor(oh, oh, rep(MI, 32), ALU.is_equal))

            first_best(M1, OH1)
            step(v.scalar_tensor_tensor(out=EL, in0=OH1, scalar=-3 * BIG, in1=EL, op0=ALU.mult, op1=ALU.add))
            first_best(M2, EQ)
            v.tensor_tensor(EX, M2, M1, ALU.subtract).then_inc(S("rt_in"), 1)
            v.tensor_tensor(AM, OH1, EQ, ALU.add).then_inc(S("picks"), 1)
            dve.wait_ge(S("rt_ex"), 2)
            step(v.tensor_reduce(GS, GX, AX.X, ALU.add))
            step(v.tensor_scalar(W1, EX, 1.0, None, ALU.add))
            step(v.tensor_tensor(W1, W1, GS, ALU.mult))
            step(v.reciprocal(W1, W1))
            step(v.tensor_tensor(W2, EX, W1, ALU.mult))
            step(v.tensor_tensor(OH1, OH1, rep(W1, 32), ALU.mult))
            step(v.tensor_tensor(EQ, EQ, rep(W2, 32), ALU.mult))
            step(v.tensor_tensor(WT, OH1, EQ, ALU.add))
            dve.wait_ge(S("pos_ps"), 1)
            dve.wait_ge(S("picks"), 1)
            step(v.tensor_scalar(TMP, ps[:, 2:4, 0:32], float(CAP), None, ALU.is_ge))
            step(v.tensor_tensor(WOV, TMP, WT, ALU.mult))
            step(v.tensor_scalar(POS, ps[:, 2:4, 0:32], 1.0, None, ALU.add))
            step(v.tensor_tensor(POS, POS, AM, ALU.mult))
            step(v.tensor_scalar(POS, POS, -1.0, None, ALU.add))
            step(v.tensor_reduce(CNT, ps[:, 4, 0:32], AX.X, ALU.max))
            v.tensor_scalar(flag[0:1, 0:1], CNT[0:1], CAP + 0.5, None, ALU.is_ge).then_inc(S("flag_set"), 1)

            for ev in ("b0_free", "b1_free", "hid_done"):
                dve.sem_inc(S(ev), 1)

            def one_hots(where):
                for t in range(TT):
                    o = OH[:, 128 * t:128 * t + 128].rearrange("p (j s) -> p j s", j=GE)
                    last = v.tensor_tensor(o, iota.unsqueeze(1).to_broadcast([P, GE, CAP]),
                                           rep(rs[:, where(128 + 32 * t)], CAP), ALU.is_equal)
                step(last)
                for t in range(TT):
                    o = OH[:, 128 * t:128 * t + 128].rearrange("p (j s) -> p j s", j=GE)
                    ow = OHW[:, 128 * t:128 * t + 128].rearrange("p (j s) -> p j s", j=GE)
                    last = v.tensor_tensor(ow, o, rep(rs[:, where(64 + 32 * t)], CAP), ALU.mult)
                last.then_inc(S("oh_done"), 1)

            def gathered(q):
                v.tensor_tensor(XS[:, 4 * q:4 * q + 4, :], ps[:, 6 + q % 2, :].rearrange("p (k s) -> p k s", k=4),
                                rep(vec("fnorm", 4 * q, 4), 128), ALU.mult).then_inc(S(f"b{q % 2}_free"), 1)

            one_hots(lambda at: slice(at, at + GE))
            for q in range(4):
                dve.wait_ge(S(f"b{q % 2}_full"), q // 2 + 1)
                gathered(q)
            with dve.Fori(0, GROUPS) as g:
                st.enter(g, 2)
                dve.wait_ge(S("b0_full"), g * 7 + 3)
                one_hots(lambda at: bass.ds(g * GE + (at + GE), GE))
                dve.wait_ge(S("sgh_done"), g + 1)
                step(v.tensor_tensor(HIDB, SG, ps[:, 0, :], ALU.mult))
                v.tensor_tensor(HIDB, HIDB, ps[:, 1, :], ALU.mult).then_inc(S("hid_done"), 1)
                for q in range(4):
                    dve.wait_ge(S(f"b{q % 2}_full"), g * 7 + (4 + q // 2))
                    gathered(q)
                for u in range(8):
                    t, nb = divmod(u, 4)
                    dve.wait_ge(S(f"b{u % 2}_full"), g * 7 + (6 + u // 2))
                    xs = x_sb[:, t, 512 * nb:512 * nb + 512]
                    last = v.tensor_tensor(xs, xs, ps[:, 6 + u % 2, :], ALU.add)
                    last.then_inc(S(f"b{u % 2}_free"), 1)
            st.leave(GROUPS)
            over = dve.value_load(flag[0:1, 0:1], min_val=0, max_val=1)
            dve.wait_ge(S("b0_free"), 7 * GROUPS + 3)
            dve.wait_ge(S("b1_free"), 7 * GROUPS + 3)
            with dve.If(over > 0):
                dve.sem_inc(S("fb_acc"), 1)
                with dve.Fori(0, NEXP) as e:
                    dve.wait_ge(S("fb_sg"), e + 1)
                    p2 = "p (b n) -> p b n"
                    v.tensor_tensor(fHID.rearrange(p2, b=2), fSG.rearrange(p2, b=2), ps[:, 0:2, :], ALU.mult)\
                        .then_inc(S("fb_silu"), 1)
                    dve.wait_ge(S("fb_silu"), e + 1)
                    v.tensor_tensor(fHID.rearrange(p2, b=2), fHID.rearrange(p2, b=2), ps[:, 2:4, :], ALU.mult)\
                        .then_inc(S("fb_hid"), 1)
                    for t in range(TT):
                        dve.wait_ge(S("fb_dn_ps"), e * 2 + (t + 2))
                        xs = x_sb[:, t, :].rearrange("p (b n) -> p b n", b=4)
                        v.scalar_tensor_tensor(out=xs, in0=ps[:, 4 * t:4 * t + 4, :],
                                               scalar=rs[:, bass.ds(e + (192 + 32 * t), 1)], in1=xs,
                                               op0=ALU.mult, op1=ALU.add).then_inc(S("fb_acc"), 1)
                        dve.wait_ge(S("fb_acc"), e * 2 + (t + 2))
                dve.nop()
            inv_rms(2)
            dve.wait_ge(S("fw_in"), 16)
            for t in range(TT):
                v.scalar_tensor_tensor(out=fout[:, t, :], in0=x_sb[:, t, :], scalar=rstd[:, 4 + t:5 + t], in1=FW,
                                       op0=ALU.mult, op1=ALU.mult).then_inc(S("fin"), 1)


_INS = ["x", "attn_norm_w", "w_in", "shift_mix", "attn_sinks", "rwkv_w0", "rwkv_w_up", "rwkv_a0", "rwkv_a_up",
        "rwkv_g_up", "rwkv_k_k", "rwkv_k_a", "rwkv_r_k", "rwkv_ln_w", "rwkv_ln_b", "w_branch_a", "w_branch_b",
        "w_out", "ffn_norm_w", "router_group_w", "router_group_b", "router_expert_w", "router_expert_b",
        "expert_w_gate", "expert_w_up", "expert_w_down", "final_norm_w"]


def kernel(**inputs):
    import numpy as _np
    import concourse.bacc as _bacc
    from concourse import mybir as _mybir
    from concourse.bass_utils import run_bass_kernel_spmd as _run

    nc = _bacc.Bacc("TRN2", target_bir_lowering=False, num_devices=1)
    arrays, aps = {}, {}
    for name in _INS:
        arrays[f"in_{name}"] = _np.ascontiguousarray(inputs[name])
    arrays["in_consts"] = constants()
    for key, arr in arrays.items():
        aps[key[3:]] = nc.dram_tensor(key, arr.shape, _mybir.dt.from_np(arr.dtype), kind="ExternalInput").ap()
    out = nc.dram_tensor("out", (1, TOK, D), F32, kind="ExternalOutput").ap()
    hybrid_layer(nc, aps, out)
    r = _run(nc, [arrays], core_ids=[0])
    return r.results[0]["out"]
```

```python
import concourse.bass as bass
from concourse import mybir
from contextlib import ExitStack

F32 = mybir.dt.float32
F32R = mybir.dt.float32r
I32 = mybir.dt.int32
ALU = mybir.AluOpType
ACT = mybir.ActivationFunctionType
AX = mybir.AxisListType

P = 128
TOK = 256
TT = TOK // P
D = 2048
KT = D // P
HD = 64
QH, KVH = 16, 4
RW = 1024
RCT = RW // P
HALVES = 2
HJ = RCT // HALVES
LORA = 64
GLORA = 160
NEXP, NGRP, EPG = 32, 4, 8
HID = 512
GE = 4
CAP = 32
GROUPS = NEXP // GE
ATTN_W, KV_W = QH * HD, KVH * HD
Z0 = ATTN_W + 2 * KV_W
LORA0 = Z0 + 3 * RW
LORA_W = 2 * LORA + GLORA
GA0 = LORA0 + LORA_W
GB0 = GA0 + D
NORM_EPS = 1e-5
GN_EPS = 64e-5
DECAY_C = -0.6065306597126334
BIG = 1e30

SLOT = 4096
RING = 4

LAG = 3

VEC_ROWS = (("anorm", 16), ("mix", 27), ("k_k", 8), ("k_a", 8), ("r_k", 8), ("a0", 8),
            ("ln_w", 8), ("ln_b", 8))
VEC = {}
_at = 0
for _name, _n in VEC_ROWS:
    VEC[_name] = _at
    _at += _n
NVEC = _at

CONST_COLS = (("ident", 128), ("tri", 256), ("upper", 128), ("ones", 128), ("blk", 128), ("mU", 64), ("mUi", 64),
              ("lvlT", 384), ("m1L", 64), ("eye", 64), ("dist", 256), ("iota", 32))
CC = {}
_at = 0
for _name, _n in CONST_COLS:
    CC[_name] = _at
    _at += _n
NCONST = _at


def constants():
    import numpy as np
    p = np.arange(P)[:, None]
    c = np.arange(P)[None, :]
    t = p % HD
    x = np.arange(HD)[None, :]
    out = np.zeros((P, NCONST), np.float32)

    def put(name, a):
        out[:, CC[name]:CC[name] + a.shape[1]] = a

    same = (p // HD) == (c // HD)
    put("ident", p == c)
    put("tri", np.concatenate([same & (p <= c), same & (p < c)], 1))
    put("upper", p < c)
    put("ones", np.ones((P, P)))
    put("blk", same)
    put("mU", t < x)
    put("mUi", t <= x)
    lv = [(t < x) & (t // (2 * b) == x // (2 * b)) & (t // b != x // b) for b in (1, 2, 4, 8, 16, 32)]
    put("lvlT", np.concatenate(lv, 1))
    put("m1L", (x < t) & (t // 2 == x // 2))
    put("eye", t == x)
    put("dist", np.concatenate([np.where(c > p, p + P - c, BIG), np.where(c <= p, p - c, BIG)], 1))
    put("iota", np.broadcast_to(np.arange(CAP)[None, :], (P, CAP)))
    return out


class Steps:

    def __init__(self, sem):
        self.sem, self.n, self.base = sem, 0, 0

    def on(self, ins):
        ins.then_inc(self.sem, 1)
        self.n += 1

    def last(self, eng):
        eng.wait_ge(self.sem, self.base + self.n)

    def enter(self, i, per):
        self.start, self.per = self.n, per
        self.base, self.n = self.start + i * per, 0

    def leave(self, count):
        assert self.n == self.per, (self.n, self.per)
        self.base, self.n = 0, self.start + count * self.per


def hybrid_layer(nc, a, out):
    with ExitStack() as ctx:
        def sb(name, shape, dt=F32):
            return ctx.enter_context(nc.sbuf_tensor(name, shape, dt))

        sems = {}

        def S(name):
            if name not in sems:
                sems[name] = ctx.enter_context(nc.semaphore(name))
            return sems[name]

        ring = sb("ring", [P, RING, SLOT])
        cst = sb("cst", [P, NCONST])
        vrow = sb("vrow", [P, P])
        vecT = sb("vecT", [P, P])
        fnorm = sb("fnorm", [P, KT])
        omm = sb("omm", [P, 27])
        omka = sb("omka", [P, 8])
        sink = sb("sink", [P, QH])
        nsm = sb("nsm", [P, 8])
        rstd = sb("rstd", [P, 6])
        amax = sb("amax", [P, 8])
        aes = sb("aes", [P, 8])
        asum = sb("asum", [P, 8])
        pend = sb("pend", [P, 16])
        gn = sb("gn", [P, 3, 16])
        flag = sb("flag", [1, 1], I32)
        rbias = sb("rbias", [P, 36])
        rs = sb("rs", [P, 1280])
        ps = ctx.enter_context(nc.psum_tensor("ps", [P, 8, 512], F32))

        def over(stack, name, shape, dt=F32R):
            return stack.enter_context(nc.sbuf_tensor(name, shape, dt))

        with ExitStack() as early:
            over(early, "below_w", [P, 15104], F32)
            w3 = [over(early, f"w_{x}", [P, 3, 1024]) for x in ("hi", "lo")]
            w1 = [over(early, f"w4_{x}", [P, 1, 1024]) for x in ("hi", "lo")]
            over(early, "below_h", [P, 1024], F32)
            h_hi, h_lo = (over(early, f"h_{x}", [P, KT, TOK]) for x in ("hi", "lo"))
        with ExitStack() as late:
            m_hi, m_lo = (over(late, f"m_{x}", [P, KT, TOK]) for x in ("hi", "lo"))
            v1_ = [over(late, f"v4_{x}", [P, 1, 1024]) for x in ("hi", "lo")]
            over(late, "below_v", [P, 25344 - 10240], F32)
            v3 = [over(late, f"v_{x}", [P, 3, 1024]) for x in ("hi", "lo")]
        arena = sb("arena", [P, 17152 + 15360])

        def C(name, n=None, at=0):
            w = dict(CONST_COLS)[name]
            return cst[:, CC[name] + at:CC[name] + at + (n or w)]

        def vec(name, i=0, n=1):
            if name == "fnorm":
                return fnorm[:, i:i + n]
            return vecT[:, VEC[name] + i:VEC[name] + i + n]

        def A(at, n):
            return arena[:, at:at + n]

        def rep(ap, n):
            return ap.unsqueeze(2).to_broadcast([ap.shape[0], ap.shape[1], n])

        def tile16(ap):
            return ap.unsqueeze(1).to_broadcast([P, 16, 64])

        HT, ZB, LZ0, LW0, AT0, T0 = 0, 4096, 10240, 11008, 15104, 17152
        hT = A(HT, 4096).rearrange("p (k t) -> p k t", k=KT)
        zT = A(ZB, 6144).rearrange("p (c t) -> p c t", c=24)
        lz = A(LZ0, 768).rearrange("p (c t) -> p c t", c=3)
        wua, g1w, g2w, w0row = (A(LW0 + 1024 * i, 1024) for i in range(4))
        attnT = A(AT0, 2048).rearrange("p (c t) -> p c t", c=8)
        yT = zT[:, 16:24, :]

        def U(i, n=1):
            return A(T0 + 1024 * i, 1024 * n)

        x_sb = U(4, 4).rearrange("p (a d) -> p a d", a=TT)
        xn = U(0, 4).rearrange("p (a d) -> p a d", a=TT)
        junk = U(0, 4).rearrange("p (a d) -> p a d", a=TT)
        probs = U(0, 2).rearrange("p (h k) -> p h k", h=8)
        probsT = U(2, 2).rearrange("p (b h q) -> p b h q", b=2, h=8)
        qT = U(4, 2).rearrange("p (c t) -> p c t", c=8)
        kTa = A(T0 + 6144, 512).rearrange("p (c t) -> p c t", c=2)
        vA = A(T0 + 6656, 512).rearrange("p (a c) -> p a c", a=TT)
        mg = U(0, 4).rearrange("p (a d) -> p a d", a=TT)
        mT = U(8, 4).rearrange("p (k t) -> p k t", k=KT)
        gates = [[A(LW0 + 1024 * (2 * b + g), 1024).rearrange("p (a n) -> p a n", a=TT) for g in range(2)] for b in range(2)]
        hfn = A(HT, 4096).rearrange("p (a d) -> p a d", a=TT)
        fout = hfn
        hfT = mT
        rw = U(14)[:, 0:576].rearrange("p (k n) -> p k n", k=KT)
        junk2 = A(ZB, 4096).rearrange("p (a d) -> p a d", a=TT)
        junk3 = A(12544, 512)
        sspart = rs[:, 1100:1108]
        XS = A(4096, 2048).rearrange("p (k s) -> p k s", k=KT)
        YS = A(6144, 2048)
        SG = A(8192, 512)
        HIDB = A(8704, 512)
        HIDT = A(9216, 512).rearrange("p (k s) -> p k s", k=4)
        OH = A(9728, 256)
        OHW = A(9984, 256)
        CTB = A(10240, 256)
        FW = A(10496, 2048)
        fSG, fHID, fHT = A(4096, 1024), A(5120, 1024), A(6144, 1024)

        gtmp = rs[:, 0:1024].rearrange("p (b n) -> p b n", b=2)
        gate_d = nc.dram_tensor("gate_spill", [P, TT, 2 * D], F32, kind="Internal").ap()
        w_in = a["w_in"][0]
        block = ctx.enter_context(nc.Block())

        def cols(c0, half, w):
            return w_in[:, c0:c0 + w].rearrange("(k p) n -> p k n", p=P)[:, 8 * half:8 * half + 8, :]

        def slot(n, w=512):
            return ring[:, n % RING, 0:8 * w].rearrange("p (k n) -> p k n", k=8)

        def pieces(b):
            return [(w1[x][:, 0, :] if b == 3 else w3[x][:, b, :]) for x in range(2)]

        def hf(x, k, t0=0, n=TOK):
            return (h_hi, h_lo)[x][:, k, t0:t0 + n]

        def late_pieces(b):
            return [(v1_[x][:, 0, :] if b == 3 else v3[x][:, b, :]) for x in range(2)]

        PRODUCTS = ((0, 0), (0, 1), (1, 0))
        UZ, UQ, UM, UO = 48, 24, 32, 32

        def z_piece(x):
            c, q = x // 4, x % 4
            return NZ + c, slot(NZ + c)[:, :, 128 * q:128 * q + 128]

        def q_piece(x):
            c, q = NQ + x // 4, x % 4
            if x < 16:
                return c, slot(c).rearrange("p k (a j n) -> p k a j n", a=2, j=4)[:, :, :, q, :], \
                    lambda o: o.rearrange("p (k a n) -> p k a n", k=8, a=2)
            if q < 2:
                return c, slot(c)[:, :, 128 * q:128 * q + 128], lambda o: o.rearrange("p (k n) -> p k n", k=8)
            return c, slot(c)[:, 4 * (q - 2):4 * (q - 2) + 4, KV_W:2 * KV_W], \
                lambda o: o.rearrange("p (k n) -> p k n", k=4)

        def v_piece(x):
            return x // 4, ring[:, x // 4 % RING, 1024 * (x % 4):1024 * (x % 4) + 1024]

        def q_buffer(x):
            return x % 3, 4 + UZ + x - 2 if x >= 3 else 4 + UZ - 4 + x + 1

        NZ = 2
        NQ = NZ + 12
        NG = NQ + 6
        NM = NG + 16
        NO = NM + 8
        NE = NO + 8
        PER_G = 24
        extra = [A(13056, SLOT), U(0, 4)]

        def eslot(c):
            s = c % 6
            if s < 2:
                return extra[s], S(f"extra_full{s}"), c // 6
            return ring[:, s - 2, :], S(f"slot_full{s - 2}"), c // 6 + NE // RING
        assert NM % RING == 0 and NO % RING == 0

        def hft_out(eng, copy, how, g, ev):
            t, kq = divmod(g, 4)
            eng.wait_ge(S("ft_ps"), g + 1)
            copy(hfT[:, 4 * kq:4 * kq + 4, 128 * t:128 * t + 128], ps[:, g, :].rearrange("p (k t) -> p k t", k=4),
                 *how).then_inc(S(ev), 1)

        @block.sync
        def _(sp):
            def load(n, dst, src, turn=0, per=0):
                if per or n >= RING:
                    sp.wait_ge(S("chunk_used"), turn * per + (n - RING + 1))
                sp.dma_start(dst, src).then_inc(S(f"slot_full{n % RING}"), 16)

            for h in range(2):
                load(h, slot(h, LORA_W), cols(LORA0, h, LORA_W))
            zc = w_in.rearrange("(k p) n -> p k n", p=P)
            for c in range(4):
                load(NZ + c, slot(NZ + c), cols(Z0 + 512 * (c // 2), c % 2, 512))
            with sp.Fori(1, 3) as i:
                for c in range(4):
                    b, h = divmod(c, 2)
                    load(NZ + c, slot(NZ + c), zc[:, 8 * h:8 * h + 8, bass.ds(i * RW + (Z0 + 512 * b), 512)], turn=i, per=4)
            for c in range(6):
                load(NQ + c, slot(NQ + c), cols(512 * (c // 2), c % 2, 512))
            for c in range(16):
                load(NG + c, slot(NG + c), cols(GA0 + 512 * (c // 2), c % 2, 512))
            wa = a["w_branch_a"][0].rearrange("(k p) n -> p k n", p=P)
            wb = a["w_branch_b"][0].rearrange("(k p) n -> p k n", p=P)
            for c in range(8):
                load(NM + c, slot(NM + c), (wa, wb)[c % 2][:, :, 512 * (c // 2):512 * (c // 2) + 512])
            wo = a["w_out"][0].rearrange("(k p) n -> p k n", p=P)
            for c in range(8):
                load(NO + c, slot(NO + c), wo[:, 8 * (c % 2):8 * (c % 2) + 8, 512 * (c // 2):512 * (c // 2) + 512])
            eg = a["expert_w_gate"][0].rearrange("e (p k) h -> p e (k h)", p=P)
            eu = a["expert_w_up"][0].rearrange("e (p k) h -> p e (k h)", p=P)
            ed = a["expert_w_down"][0].rearrange("e (k p) n -> p e k n", p=P)

            def eload(c, first, used):
                dst, full, _ = eslot(c)
                if c < 16:
                    src = (eu if c % 2 else eg)[:, bass.ds(first, GE), 2 * HID * (c // 2):2 * HID * (c // 2 + 1)]
                else:
                    kh, nh = divmod(c - 16, 2)
                    src = ed[:, bass.ds(first, GE), kh, 1024 * nh:1024 * nh + 1024]
                if used is not None:
                    sp.wait_ge(S("chunk_used"), used)
                sp.dma_start(dst.rearrange("p (j n) -> p j n", j=GE), src).then_inc(full, 16)

            sp.wait_ge(S("mg_done"), 4)
            eload(0, 0, None)
            sp.wait_ge(S("mtr_ps"), 8)
            eload(1, 0, None)
            for c in range(2, PER_G):
                eload(c, 0, NE + c - 5 if c >= 6 else NE - RING + c - 2 + 1)
            with sp.Fori(1, GROUPS) as g:
                first = sp.snap(g * GE)
                for c in range(PER_G):
                    eload(c, first, g * PER_G + (NE + c - 5))
            sp.wait_ge(S("flag_set"), 1)
            over = sp.value_load(flag[0:1, 0:1], min_val=0, max_val=1)
            with sp.If(over > 0):
                sp.wait_ge(S("chunk_used"), NE + PER_G * GROUPS)
                with sp.Fori(0, NEXP) as e:
                    sp.wait_ge(S("fb_dn_ps"), e * 2 + 1)
                    for s in range(4):
                        w = (eg if s < 2 else eu)[:, bass.ds(e, 1), SLOT * (s % 2):SLOT * (s % 2) + SLOT]
                        sp.dma_start(ring[:, s, :], w.rearrange("p e n -> p (e n)")).then_inc(S("fb_up_in"), 16)
                    sp.wait_ge(S("fb_up_used"), e + 1)
                    for s in range(2):
                        w = ed[:, bass.ds(e, 1), 2 * s:2 * s + 2, :]
                        sp.dma_start(ring[:, s, :].rearrange("p (k n) -> p k n", k=2),
                                     w.rearrange("p e k n -> p (e k) n")).then_inc(S("fb_down_in"), 16)
                sp.nop()
            for t in range(TT):
                sp.wait_ge(S("fin"), t + 1)
                sp.dma_start(out[0].rearrange("(a p) d -> p a d", p=P)[:, t, :], fout[:, t, :]).then_inc(S("stored"), 16)
            sp.wait_ge(S("stored"), 16 * TT)

        @block.gpsimd
        def _(pool):
            pool.memset(vrow[:, :], 0.0).then_inc(S("vrow_zero"), 1)
            pool.wait_ge(S("const_in"), 16)
            for hh in range(HALVES):
                pool.wait_ge(S("lt_done"), hh + 1)
                for lv in range(1, 6):
                    if lv > 1:
                        pool.wait_ge(S("v1_ps"), 10 * hh + 2 * (lv - 1))
                    pool.tensor_tensor(U(6).rearrange("p (g x) -> p g x", g=16),
                                       U(8).rearrange("p (g x) -> p g x", g=16),
                                       tile16(C("lvlT", 64, 64 * lv)), ALU.mult).then_inc(S("ltm_done"), 1)

            pool.wait_ge(S("y_done"), HALVES)
            for t in range(TT):
                pool.wait_ge(S(f"gate_stored{t}"), 16 * 8)
            for nb in range(4):
                if nb >= 2:
                    pool.wait_ge(S("mg_done"), nb - 1)
                for g in range(2):
                    pool.dma_start(gates[nb % 2][g], gate_d[:, :, D * g + 512 * nb:D * g + 512 * nb + 512])\
                        .then_inc(S(f"gate_in{nb % 2}"), 16)

        @block.tensor
        def _(pe):
            mm = nc.tensor.matmul

            def full(n, turn=0, per=0):
                pe.wait_ge(S(f"slot_full{n % RING}"), turn * (16 * per // RING) + 16 * (n // RING + 1))

            def tp(o, i):
                return nc.tensor.transpose(o, i, C("ident")[0:i.shape[0], 0:i.shape[0]])

            def transposes(src, ev):
                for g in range(8):
                    t, kq = divmod(g, 4)
                    for q in range(4):
                        k = 4 * kq + q
                        last = tp(ps[:, g, 128 * q:128 * q + 128], src[:, t, 128 * k:128 * k + 128])
                    last.then_inc(S(ev), 1)

            pe.wait_ge(S("const_in"), 16)
            pe.wait_ge(S("vec_in"), 16 * 11)
            tp(ps[:, 0, 0:NVEC], vrow[0:NVEC, :]).then_inc(S("vt_ps"), 1)
            pe.wait_ge(S("vt_done"), 1)
            pe.wait_ge(S("xn_done"), 2)
            transposes(xn, "xt_ps")
            pe.wait_ge(S("ht_done"), 8)

            full(0)
            full(1)
            for t, m in enumerate((128, 128, 32)):
                for k in range(KT):
                    last = mm(ps[0:m, 4 + t, 0:TOK], slot(k // 8, LORA_W)[:, k % 8, 128 * t:128 * t + m], hT[:, k, :],
                              start=k == 0, stop=k == KT - 1)
                    if t == 2 and k % 8 == 7:
                        last.then_inc(S("chunk_used"), 1)
                if t < 2:
                    last.then_inc(S("z_ps"), 1)
            def unit(buf, out, ks, start, stop):
                hi, lo = pieces(buf)
                for n, k in enumerate(ks):
                    for p, (w, x) in enumerate(PRODUCTS):
                        last = mm(out, (hi, lo)[w][:, 128 * n:128 * n + 128], hf(x, k),
                                  start=start and n == 0 and p == 0, stop=stop and n == 7 and p == 2)
                return last

            pe.wait_ge(S("h_lo_done"), 1)
            with pe.Fori(0, 3) as i:
                for x in range(16):
                    b, h, c = x // 8, x // 4 % 2, x % 4
                    if x % 8 == 0:
                        pe.wait_ge(S("z_done"), i * 8 + (1 + 2 * b))
                    pe.wait_ge(S("w_lo"), i * 16 + (x + 1))
                    unit(x % 4, ps[:, 4 * b + c, 0:TOK], range(8 * h, 8 * h + 8), h == 0, h == 1)\
                        .then_inc(S("w_used"), 1)
            for x in range(UQ):
                c = x % 4
                b, h = divmod(x // 4, 2)
                if x in (0, 8):
                    pe.wait_ge(S("z_done"), (23, 27)[b])
                if x == 16:
                    pe.wait_ge(S("qkv_done"), 4)
                pe.wait_ge(S("w_lo"), UZ + x + 1)
                buf = q_buffer(x)[0]
                if b < 2 or c < 2:
                    last = unit(buf, ps[:, 4 * (b % 2) + c, 0:TOK], range(8 * h, 8 * h + 8), h == 0, h == 1)
                else:
                    for k in range(4):
                        kk = 8 * h + 4 * (c - 2) + k
                        for t in range(TT):
                            for p, (w, y) in enumerate(PRODUCTS):
                                last = mm(ps[:, 2 + t, 0:KV_W], hf(y, kk, 128 * t, 128),
                                          pieces(buf)[w][:, KV_W * k:KV_W * k + KV_W],
                                          start=kk == 0 and p == 0, stop=kk == KT - 1 and p == 2)
                last.then_inc(S("w_used"), 1)

            gate_part = [0]

            def gate_mm(count):
                for m in range(gate_part[0], gate_part[0] + count):
                    tile, k = divmod(m, KT)
                    b, t = divmod(tile, TT)
                    n = NG + 2 * b + k // 8
                    if k == 0 and tile:
                        pe.wait_ge(S("gate_out"), tile)
                    if k % 8 == 0:
                        full(n)
                    last = mm(ps[:, 7, :], hT[:, k, 128 * t:128 * t + 128], slot(n)[:, k % 8, :],
                              start=k == 0, stop=k == KT - 1)
                    if t and k % 8 == 7:
                        last.then_inc(S("chunk_used"), 1)
                    elif k == KT - 1:
                        last.then_inc(S("gate_ps"), 1)
                gate_part[0] += count

            def gate_half():
                gate_mm(8)

            sc = ps[:, 0:4, :].rearrange("p b (j k) -> p (b j) k", j=2)
            pt = [ps[:, 4:6, :].rearrange("p b (h q) -> p (b h) q", h=4),
                  ps[:, 2:4, :].rearrange("p b (h q) -> p (b h) q", h=4)]
            pe.wait_ge(S("qkv_done"), 12)
            for u in range(4):
                n, hg = divmod(u, 2)
                if u:
                    pe.wait_ge(S("pv_done"), u)
                for j in range(4):
                    for hp in range(2):
                        r = slice(64 * hp, 64 * hp + 64)
                        last = mm(sc[:, 4 * hp + j, 0:128 * (n + 1)], qT[r, 4 * hg + j, 128 * n:128 * n + 128],
                                  kTa[r, hg, 0:128 * (n + 1)], start=True, stop=True)
                last.then_inc(S("sc_ps"), 1)
                gate_half()
                if u >= 2:
                    gate_half()
                pe.wait_ge(S("pr_done"), u + 1)
                for kb in range(n + 1):
                    for h in range(8):
                        last = tp(pt[kb][:, h, :], probs[:, h, 128 * kb:128 * kb + 128])
                last.then_inc(S("pt_ps"), 1)
                gate_half()
                pe.wait_ge(S("pt_done"), (1, 2, 4, 6)[u])
                for h in range(8):
                    hp, j = divmod(h, 4)
                    kv = 2 * hg + hp
                    o = ps[64 * (j % 2):64 * (j % 2) + 64, 0, 128 * (2 * hp + j // 2):128 * (2 * hp + j // 2) + 128]
                    for kb in range(n + 1):
                        last = mm(o, vA[:, kb, 64 * kv:64 * kv + 64], probsT[:, kb, h, :], start=kb == 0, stop=kb == n)
                last.then_inc(S("pv_ps"), 1)

            def blk(ap, hp, ci, j, w=64):
                o = w * (8 * hp + 4 * ci + j)
                return ap[:, o:o + w]

            pairs = [(cp, hp, ci, j) for ci in range(2) for j in range(4) for hp in range(2) for cp in range(2)]
            quads = [(cp, ci, j) for ci in range(2) for j in range(4) for cp in range(2)]
            pe.wait_ge(S("lora_done"), 3)
            pe.wait_ge(S("small_in"), 16 * 7)
            for hh in range(HALVES):
                AR = U(0, 2).rearrange("p (j w t) -> p j w t", j=HJ, w=2)
                BT = U(2).rearrange("p (j t) -> p j t", j=HJ)
                KTT = U(3).rearrange("p (j t) -> p j t", j=HJ)
                MVA = U(4, 2)
                UA = U(12, 2)
                if hh:
                    pe.wait_ge(S("y_done"), hh)
                else:
                    pe.wait_ge(S("pv_done"), 4)
                hc = 512 * hh
                for t in range(TT):
                    mm(ps[:, t, :], lz[0:64, 0, 128 * t:128 * t + 128], wua[0:64, hc:hc + 512], start=True, stop=False)
                    last = mm(ps[:, t, :], C("ones")[0:1, :], w0row[0:1, hc:hc + 512], start=False, stop=True)
                last.then_inc(S("wl_ps"), 1)
                for j in range(HJ):
                    last = mm(ps[:, 2 + j // 2, 256 * (j % 2):256 * (j % 2) + 256],
                              wua[64:128, hc + 128 * j:hc + 128 * j + 128], lz[64:128, 0, :], start=True, stop=True)
                last.then_inc(S("a_ps"), 1)
                if hh == 0:
                    gate_half()
                pe.wait_ge(S("sg_done"), hh + 1)
                for j in range(HJ):
                    for t in range(TT):
                        last = mm(ps[:, (4, 5, 6, 0)[j], 256 * t:256 * t + 256],
                                  U(4)[:, 512 * t + 128 * j:512 * t + 128 * j + 128], C("tri"), start=True, stop=True)
                last.then_inc(S("cum_ps"), 1)
                pe.wait_ge(S("sq_done"), hh + 1)
                pe.wait_ge(S("a_done"), hh + 1)
                for b in range(2):
                    last = mm(ps[:, 1 + b, :], C("blk"), U(7)[:, 512 * b:512 * b + 512], start=True, stop=True)
                last.then_inc(S("ks_ps"), 1)
                if hh == 0:
                    gate_half()
                pe.wait_ge(S("nrm_done"), hh + 1)
                for ci in range(2):
                    for j in range(HJ):
                        last = tp(ps[:, 2 + ci, 128 * j:128 * j + 128], yT[:, HJ * hh + j, 128 * ci:128 * ci + 128])
                last.then_inc(S("vtr_ps"), 1)
                gate_half()
                pe.wait_ge(S("rk_done"), hh + 1)
                pe.wait_ge(S("P_done"), hh + 1)
                for b in range(2):
                    last = mm(ps[:, 4 + b, :], C("blk"), U(12)[:, 512 * b:512 * b + 512], start=True, stop=True)
                last.then_inc(S("bon_ps"), 1)
                gate_half()
                gate_half()

                def tk(ap, c):
                    return ap[:, 64 * c:64 * c + 64]

                pe.wait_ge(S("arbk"), hh + 1)
                pe.wait_ge(S("vt2_done"), hh + 1)
                pe.wait_ge(S("bon_done"), hh + 1)
                for cp, hp, ci, j in pairs:
                    r, q, c = slice(64 * hp, 64 * hp + 64), slice(64 * cp, 64 * cp + 64), 2 * ci + cp
                    last = mm(ps[q, hp, 256 * ci + 64 * j:256 * ci + 64 * j + 64], tk(AR[r, j, 0, :], c), tk(BT[r, j, :], c),
                              start=True, stop=True)
                last.then_inc(S("l_ps"), 1)
                for cp, hp, ci, j in pairs:
                    r, q, c = slice(64 * hp, 64 * hp + 64), slice(64 * cp, 64 * cp + 64), 2 * ci + cp
                    last = mm(ps[q, 2 + 2 * hp + ci, 128 * j:128 * j + 128], tk(BT[r, j, :], c),
                              AR[r, j, :, 64 * c:64 * c + 64], start=True, stop=True)
                last.then_inc(S("lt_ps"), 1)
                gate_half()
                pe.wait_ge(S("x0_done"), hh + 1)
                pe.wait_ge(S("lt_done"), hh + 1)
                for cp, hp, ci, j in pairs:
                    r, q, c = slice(64 * hp, 64 * hp + 64), slice(64 * cp, 64 * cp + 64), 2 * ci + cp
                    last = mm(ps[q, 2 * hp + ci, 128 * j:128 * j + 128], tk(KTT[r, j, :], c),
                              AR[r, j, :, 64 * c:64 * c + 64], start=True, stop=True)
                last.then_inc(S("mt_ps"), 1)
                for ci in range(2):
                    for j in range(HJ):
                        last = tp(ps[:, 4 + ci, 128 * j:128 * j + 128], AR[:, j, 0, 128 * ci:128 * ci + 128])
                last.then_inc(S("at_ps"), 1)
                pe.wait_ge(S("mt_done"), hh + 1)
                for ci in range(2):
                    for j in range(HJ):
                        last = tp(ps[:, ci, 128 * j:128 * j + 128], BT[:, j, 128 * ci:128 * ci + 128])
                last.then_inc(S("bt_ps"), 1)
                for cp, hp, ci, j in pairs:
                    q = slice(64 * cp, 64 * cp + 64)
                    last = mm(ps[q, 2 + hp, 256 * ci + 64 * j:256 * ci + 64 * j + 64], blk(U(10), hp, ci, j)[q],
                              blk(U(7), hp, ci, j)[q], start=True, stop=True)
                last.then_inc(S("mv_ps"), 1)
                pe.wait_ge(S("at_done"), hh + 1)
                for ci in range(2):
                    for j in range(HJ):
                        last = tp(ps[:, 4 + ci, 128 * j:128 * j + 128], KTT[:, j, 128 * ci:128 * ci + 128])
                last.then_inc(S("kt_ps"), 1)
                pe.wait_ge(S("bt_done"), hh + 1)
                for lv in range(1, 6):
                    pe.wait_ge(S("ltm_done"), 5 * hh + lv)
                    for hp in range(2):
                        pe.wait_ge(S("x_done"), 10 * hh + 2 * (lv - 1) + hp + 1)
                        for cp, ci, j in quads:
                            q = slice(64 * cp, 64 * cp + 64)
                            last = mm(ps[q, hp, 256 * ci + 64 * j:256 * ci + 64 * j + 64], blk(U(6), hp, ci, j)[q],
                                      blk(U(12), hp, ci, j)[q], start=True, stop=True)
                        last.then_inc(S("v1_ps"), 1)
                    gate_mm((3, 3, 3, 3, 4)[lv - 1])
                    if lv == 1:
                        pe.wait_ge(S("mv_done"), hh + 1)
                        pe.wait_ge(S("kt_done"), hh + 1)
                    for w, ev in ((0, "w_ps"), (1, "wt_ps"))[lv == 5:]:
                        for hp in range(2):
                            if not w or lv == 5:
                                pe.wait_ge(S("v1_done"), 10 * hh + 2 * (lv - 1) + hp + 1)
                            pe.wait_ge(S("xt_done"), 12 * hh + 2 * (lv - 1) + hp + 1)
                            for cp, ci, j in quads:
                                q = slice(64 * cp, 64 * cp + 64)
                                o = slice(256 * ci + 64 * j, 256 * ci + 64 * j + 64)
                                v1, xt = blk(U(14), hp, ci, j)[q], blk(U(13), hp, ci, j)[q]
                                if w:
                                    last = mm(ps[q, 4 + hp, o], v1, xt, start=True, stop=True)
                                else:
                                    last = mm(ps[q, 2 + hp, o], xt, v1, start=True, stop=True)
                            last.then_inc(S(ev), 1)
                pe.wait_ge(S("xt_done"), 12 * hh + 12)
                for cp, hp, ci, j in pairs:
                    q = slice(64 * cp, 64 * cp + 64)
                    last = mm(ps[q, 2 + 2 * hp + ci, 128 * j:128 * j + 128], blk(U(13), hp, ci, j)[q],
                              blk(MVA, hp, ci, j, 128)[q], start=True, stop=True)
                last.then_inc(S("ua_ps"), 1)
                pe.wait_ge(S("ua_done"), hh + 1)

                def nU(hp, ci, j):
                    return blk(UA, hp, ci, j, 128)[:, 0:64]

                def nA(hp, ci, j):
                    return blk(UA, hp, ci, j, 128)[:, 64:128]

                for cp, hp, ci, j in pairs:
                    q, r, o = slice(64 * cp, 64 * cp + 64), slice(64 * hp, 64 * hp + 64), slice(256 * ci + 64 * j, 256 * ci + 64 * j + 64)
                    last = mm(ps[r, cp, o], nA(hp, ci, j)[q], blk(U(9), hp, ci, j)[q], start=True, stop=True)
                last.then_inc(S("rb_ps"), 1)
                for cp, hp, ci, j in pairs:
                    q, r, o = slice(64 * cp, 64 * cp + 64), slice(64 * hp, 64 * hp + 64), slice(256 * ci + 64 * j, 256 * ci + 64 * j + 64)
                    last = mm(ps[r, 2 + cp, o], nA(hp, ci, j)[q], blk(U(2), hp, ci, j)[q], start=True, stop=True)
                last.then_inc(S("g_ps"), 1)
                for cp, hp, ci, j in pairs:
                    q, r, o = slice(64 * cp, 64 * cp + 64), slice(64 * hp, 64 * hp + 64), slice(256 * ci + 64 * j, 256 * ci + 64 * j + 64)
                    mm(ps[r, 4 + cp, o], blk(U(3), hp, ci, j)[q], blk(U(7), hp, ci, j)[q], start=True, stop=False)
                    last = mm(ps[r, 4 + cp, o], blk(U(2), hp, ci, j)[q], nU(hp, ci, j)[q], start=False, stop=True)
                last.then_inc(S("f_ps"), 1)
                gate_half()
                pe.wait_ge(S("rb_done"), hh + 1)
                for cp, hp, ci, j in pairs:
                    q, o = slice(64 * cp, 64 * cp + 64), slice(256 * ci + 64 * j, 256 * ci + 64 * j + 64)
                    mm(ps[q, hp, o], blk(U(11), hp, ci, j)[q], blk(U(7), hp, ci, j)[q], start=True, stop=False)
                    last = mm(ps[q, hp, o], blk(U(9), hp, ci, j)[q], nU(hp, ci, j)[q], start=False, stop=True)
                last.then_inc(S("y0_ps"), 1)
                pe.wait_ge(S("g_done"), hh + 1)
                pe.wait_ge(S("f_done"), hh + 1)

                def state(c, hp, j):
                    s = U(14)[:, 0:256] if c == 1 else U(6)[:, 256 * (c - 2):256 * (c - 2) + 256]
                    return s[64 * hp:64 * hp + 64, 64 * j:64 * j + 64]

                for c in (1, 2):
                    ci, cp = divmod(c, 2)
                    if c > 1:
                        pe.wait_ge(S("s_done"), 2 * hh + c - 1)
                    for j in range(HJ):
                        for hp in range(2):
                            r = slice(64 * hp, 64 * hp + 64)
                            o = 512 * cp + 256 * ci + 64 * j
                            last = mm(ps[r, 6, 256 * (c - 1) + 64 * j:256 * (c - 1) + 64 * j + 64], U(10)[r, o:o + 64], state(c, hp, j),
                                      start=True, stop=True)
                    last.then_inc(S("s_ps"), 1)
                    if c == 1:
                        gate_half()
                pe.wait_ge(S("s_done"), 2 * hh + 2)
                for c in (1, 2, 3):
                    ci, cp = divmod(c, 2)
                    for j in range(HJ):
                        for hp in range(2):
                            r = slice(64 * hp, 64 * hp + 64)
                            last = mm(ps[64 * cp:64 * cp + 64, 2 + hp, 256 * ci + 64 * j:256 * ci + 64 * j + 64],
                                      tk(AR[r, j, 1, :], c), state(c, hp, j), start=True, stop=True)
                last.then_inc(S("yy_ps"), 1)
                gate_half()
                gate_half()
                pe.wait_ge(S("y0_done"), hh + 1)
                for j in range(HJ):
                    o = ps[:, 4 + j // 2, 256 * (j % 2):256 * (j % 2) + 256]
                    mm(o, g1w[:, hc + 128 * j:hc + 128 * j + 128], lz[:, 1, :], start=True, stop=False)
                    last = mm(o, g2w[0:32, hc + 128 * j:hc + 128 * j + 128], lz[0:32, 2, :], start=False, stop=True)
                last.then_inc(S("gt_ps"), 1)
                pe.wait_ge(S("yn_done"), hh + 1)
                for j in range(HJ):
                    for ci in range(2):
                        last = tp(ps[:, j // 2, 256 * (j % 2) + 128 * ci:256 * (j % 2) + 128 * ci + 128],
                                  U(4)[:, 512 * ci + 128 * j:512 * ci + 128 * j + 128])
                last.then_inc(S("ynt_ps"), 1)

            assert gate_part[0] == 16 * KT
            def late_unit(buf, bank, ks, start, stop):
                for t in range(TT):
                    for n, k in enumerate(ks):
                        for p, (w, x) in enumerate(PRODUCTS):
                            last = mm(ps[:, bank + t, :], (m_hi, m_lo)[x][:, k, 128 * t:128 * t + 128],
                                      late_pieces(buf)[w][:, 512 * n:512 * n + 512],
                                      start=start and n == 0 and p == 0, stop=stop and n == 1 and p == 2)
                last.then_inc(S("v_used"), 1)

            pe.wait_ge(S("m_lo_done"), 3)
            with pe.Fori(0, 2) as i:
                for x in range(16):
                    c, q = divmod(x, 4)
                    b, g = divmod(c, 2)
                    if q == 0:
                        pe.wait_ge(S(("m1_done", "m2_done")[g]), i * 2 + (b + 1))
                    pe.wait_ge(S("v_lo"), i * 16 + (x + 1))
                    late_unit(x % 4, 2 * g, range(8 - 8 * g + 2 * q, 8 - 8 * g + 2 * q + 2), q == 0, q == 3)
            pe.wait_ge(S("mg_done"), 4)
            transposes(mg, "mtr_ps")
            pe.wait_ge(S("m_lo_done"), 3 + 8)
            for x in range(UO):
                c, q = divmod(x, 4)
                nb, h = divmod(c, 2)
                pe.wait_ge(S("v_lo"), UM + x + 1)
                late_unit(x % 4, 2 * nb, range(8 * h + 2 * q, 8 * h + 2 * q + 2), h == 0 and q == 0, h == 1 and q == 3)

            pe.wait_ge(S("x2_done"), 4)
            for g in range(8):
                t, kq = divmod(g, 4)
                for q in range(4):
                    last = tp(ps[:, g, 128 * q:128 * q + 128],
                              x_sb[:, t, :].rearrange("q (p k) -> q k p", k=KT)[:, 4 * kq + q, :])
                last.then_inc(S("ft_ps"), 1)
            pe.wait_ge(S("rw_scaled"), 1)
            for t in range(TT):
                pe.wait_ge(S("hft_act"), 2 * t + 2)
                pe.wait_ge(S("hft_dve"), 2 * t + 2)
                for k in range(KT):
                    last = mm(ps[:, t, 0:36], hfT[:, k, 128 * t:128 * t + 128], rw[:, k, :], start=k == 0, stop=k == KT - 1)
            last.then_inc(S("lg_ps"), 1)
            pe.wait_ge(S("picks"), 1)
            AM = rs[:, 0:64].rearrange("p (a e) -> p a e", a=TT)
            mm(ps[:, 2, 0:32], C("upper"), AM[:, 0, :], start=True, stop=True)
            mm(ps[:, 3, 0:32], C("upper"), AM[:, 1, :], start=True, stop=False)
            mm(ps[:, 3, 0:32], C("ones"), AM[:, 0, :], start=False, stop=True)
            mm(ps[:, 4, 0:32], C("ones"), AM[:, 0, :], start=True, stop=False)
            mm(ps[:, 4, 0:32], C("ones"), AM[:, 1, :], start=False, stop=True).then_inc(S("pos_ps"), 1)
            pe.wait_ge(S("flag_set"), 1)
            pe.wait_ge(S("hfn_done"), 2)

            def gather(q, b_free):
                pe.wait_ge(S(f"b{q % 2}_free"), b_free)
                for k in range(4):
                    for t in range(TT):
                        last = mm(ps[:, 6 + q % 2, 128 * k:128 * k + 128],
                                  hfn[:, t, 512 * q + 128 * k:512 * q + 128 * k + 128], OH[:, 128 * t:128 * t + 128],
                                  start=t == 0, stop=t == 1)
                last.then_inc(S(f"b{q % 2}_full"), 1)

            pe.wait_ge(S("oh_done"), 1)
            for q in range(4):
                gather(q, q // 2 + 1)
            with pe.Fori(0, GROUPS) as g:
                pe.wait_ge(S("b0_free"), g * 7 + 3)
                pe.wait_ge(S("b1_free"), g * 7 + 3)
                pe.wait_ge(S("hid_done"), g + 1)
                for c in range(16):
                    w, sem, before = eslot(c)
                    pe.wait_ge(sem, g * 64 + 16 * (before + 1))
                    w = w.rearrange("p (j k h) -> p j k h", j=GE, k=2)
                    for kk in range(2):
                        k = 2 * (c // 2) + kk
                        for j in range(GE):
                            last = mm(ps[32 * j:32 * j + 32, c % 2, :], XS[:, k, 32 * j:32 * j + 32], w[:, j, kk, :],
                                      start=k == 0, stop=k == KT - 1, tile_position=(0, 32 * j))
                    last.then_inc(S("chunk_used"), 1)
                    if c == 3:
                        for t in range(TT):
                            last = tp(ps[:, 6, 128 * t:128 * t + 128], OHW[:, 128 * t:128 * t + 128])
                        last.then_inc(S("b0_full"), 1)
                pe.wait_ge(S("hid_done"), g + 2)
                for k in range(4):
                    last = tp(ps[:, 7, 128 * k:128 * k + 128], HIDB[:, 128 * k:128 * k + 128])
                last.then_inc(S("b1_full"), 1)
                pe.wait_ge(S("b1_free"), g * 7 + 4)
                pe.wait_ge(S("ys_done"), g + 1)
                for c in range(8):
                    kh, nh = divmod(c, 2)
                    w, sem, before = eslot(16 + c)
                    pe.wait_ge(sem, g * 64 + 16 * (before + 1))
                    w = w.rearrange("p (j n) -> p j n", j=GE)
                    for nb in range(2):
                        for j in range(GE):
                            last = mm(ps[32 * j:32 * j + 32, 2 + 2 * nh + nb, :], HIDT[:, kh, 32 * j:32 * j + 32],
                                      w[:, j, 512 * nb:512 * nb + 512], start=kh == 0, stop=kh == 3,
                                      tile_position=(0, 32 * j))
                    last.then_inc(S("chunk_used"), 1)
                    if c == 1:
                        pe.wait_ge(S("oh_done"), g + 2)
                    if 1 <= c < 5:
                        gather(c - 1, g * 7 + (4 + (c - 1) // 2))
                pe.wait_ge(S("ys_done"), g + 2)
                for u in range(8):
                    t, nb = divmod(u, 4)
                    pe.wait_ge(S(f"b{u % 2}_free"), g * 7 + (6 + u // 2))
                    mm(ps[:, 6 + u % 2, :], CTB[:, 128 * t:128 * t + 128], YS[:, 512 * nb:512 * nb + 512],
                       start=True, stop=True).then_inc(S(f"b{u % 2}_full"), 1)

            over = pe.value_load(flag[0:1, 0:1], min_val=0, max_val=1)
            with pe.If(over > 0):
                pe.wait_ge(S("b0_free"), 7 * GROUPS + 3)
                pe.wait_ge(S("b1_free"), 7 * GROUPS + 3)
                pe.sem_inc(S("fb_dn_ps"), 1)
                with pe.Fori(0, NEXP) as e:
                    pe.wait_ge(S("fb_up_in"), e * 64 + 64)
                    pe.wait_ge(S("fb_acc"), e * 2 + 1)
                    for w in range(2):
                        for t in range(TT):
                            for k in range(KT):
                                last = mm(ps[:, 2 * w + t, :], hfT[:, k, 128 * t:128 * t + 128],
                                          slot(2 * w + k // 8)[:, k % 8, :], start=k == 0, stop=k == KT - 1)
                    last.then_inc(S("fb_up_used"), 1)
                    pe.wait_ge(S("fb_hid"), e + 1)
                    for t in range(TT):
                        for k in range(4):
                            last = tp(ps[:, 4 + t, 128 * k:128 * k + 128], fHID[:, 512 * t + 128 * k:512 * t + 128 * k + 128])
                    last.then_inc(S("fb_ht_ps"), 1)
                    pe.wait_ge(S("fb_ht"), e + 1)
                    pe.wait_ge(S("fb_down_in"), e * 32 + 32)
                    for t in range(TT):
                        for nb in range(4):
                            for k in range(4):
                                last = mm(ps[:, 4 * t + nb, :], fHT[:, 512 * t + 128 * k:512 * t + 128 * k + 128],
                                          ring[:, k // 2, 2048 * (k % 2) + 512 * nb:2048 * (k % 2) + 512 * nb + 512],
                                          start=k == 0, stop=k == 3)
                        last.then_inc(S("fb_dn_ps"), 1)
                pe.nop()

        @block.scalar
        def _(act):
            f = nc.scalar.activation
            xv = a["x"][0].rearrange("(a p) d -> p a d", p=P)
            for t in range(TT):
                act.dma_start(x_sb[:, t, :], xv[:, t, :]).then_inc(S(f"x_in{t}"), 16)
            act.dma_start(cst[:, :], a["consts"]).then_inc(S("const_in"), 16)
            act.wait_ge(S("vrow_zero"), 1)

            def rows(name, src, at=0, n=None):
                r = VEC[name] + at
                act.dma_start(vrow[r:r + n, 0:src.shape[-1]], src).then_inc(S("vec_in"), 16)

            rows("anorm", a["attn_norm_w"][0].rearrange("(k p) -> k p", p=P), n=16)
            act.dma_start(fnorm[:, :], a["ffn_norm_w"][0].rearrange("(p k) -> p k", p=P)).then_inc(S("vec_in"), 16)
            mixw = a["shift_mix"]
            rows("mix", mixw[0, 3 * RW:3 * RW + 256].rearrange("(k p) -> k p", p=P), n=2)
            rows("mix", mixw[0:1, 3 * RW + 256:3 * RW + 288], at=2, n=1)
            rows("mix", mixw[0, 0:3 * RW].rearrange("(k p) -> k p", p=P), at=3, n=24)
            for name, key in (("k_k", "rwkv_k_k"), ("k_a", "rwkv_k_a"), ("a0", "rwkv_a0"), ("ln_w", "rwkv_ln_w"),
                              ("ln_b", "rwkv_ln_b")):
                rows(name, a[key][0].rearrange("(k p) -> k p", p=P), n=8)
            act.dma_start(vrow[VEC["r_k"]:VEC["r_k"] + 8, :], a["rwkv_r_k"][0].rearrange("(k h) d -> k (h d)", h=2))\
                .then_inc(S("vec_in"), 16)
            act.dma_start(sink[:, :], a["attn_sinks"][0].partition_broadcast(P)).then_inc(S("small_in"), 16)
            act.dma_start(wua[0:64, :], a["rwkv_w_up"][0]).then_inc(S("small_in"), 16)
            act.dma_start(wua[64:128, :], a["rwkv_a_up"][0]).then_inc(S("small_in"), 16)
            act.dma_start(g1w[:, :], a["rwkv_g_up"][0, 0:128, :]).then_inc(S("small_in"), 16)
            act.dma_start(g2w[0:32, :], a["rwkv_g_up"][0, 128:160, :]).then_inc(S("small_in"), 16)
            act.dma_start(w0row[0:1, :], a["rwkv_w0"]).then_inc(S("small_in"), 16)
            act.dma_start(rbias[:, 0:4], a["router_group_b"][0].partition_broadcast(P)).then_inc(S("small_in"), 16)
            act.dma_start(rbias[:, 4:36], a["router_expert_b"][0].partition_broadcast(P)).then_inc(S("rb_in"), 16)

            def squares(src, dst, ev):
                for t in range(TT):
                    f(dst[:, t, :], src[:, t, :], ACT.Square, accum_out=rstd[:, t:t + 1]).then_inc(S(ev), 1)

            for t in range(TT):
                act.wait_ge(S(f"x_in{t}"), 16)
            squares(x_sb, junk, "ss_done")
            act.wait_ge(S("ms_done"), 1)
            f(rstd[:, 2:4], rstd[:, 2:4], ACT.Sqrt).then_inc(S("rt_done"), 1)

            act.wait_ge(S("vt_done"), 1)
            act.wait_ge(S("ht_done"), 8)
            f(h_hi[:, :, :], hT, ACT.Copy).then_inc(S("h_hi_done"), 1)
            for t, m in enumerate((128, 128, 32)):
                act.wait_ge(*((S("z_ps"), t + 1) if t < 2 else (S("chunk_used"), NZ)))
                f(lz[0:m, t, :], ps[0:m, 4 + t, 0:TOK], ACT.Copy, scale=omm[0:m, t:t + 1]).then_inc(S("za_done"), 1)
            def z_out(e, i):
                c = 4 * (e // 8) + e % 4
                act.wait_ge(S("w_used"), i * 16 + (4 + e + 1))
                f(zT[:, bass.ds(i * 8 + c, 1), :].rearrange("p a t -> p (a t)"), ps[:, c, 0:TOK], ACT.Copy,
                  scale=omm[:, bass.ds(i * 8 + 3 + c, 1)]).then_inc(S("za_done"), 1)

            def z_hi(x, i):
                n, src = z_piece(x)
                if x % 4 == 0:
                    act.wait_ge(S(f"slot_full{n % RING}"), i * 16 + 16 * (n // RING + 1))
                act.wait_ge(S("w_used"), i * 16 + (x + 1))
                f(pieces(x % 4)[0].rearrange("p (k n) -> p k n", k=8), src, ACT.Copy).then_inc(S("w_hi"), 1)

            for x in range(LAG):
                z_hi(x, 0)
            with act.Fori(0, 2) as i:
                for x in range(LAG, 16 + LAG):
                    z_hi(x, i)
                    if (x - LAG) % 8 >= 4:
                        z_out(x - LAG, i)
            for x in range(LAG, 16):
                z_hi(x, 2)
                if (x - LAG) % 8 >= 4:
                    z_out(x - LAG, 2)
            act.wait_ge(S("z_done"), 3)
            f(lz[0:64, 0, :], lz[0:64, 0, :], ACT.Tanh).then_inc(S("lora_done"), 1)
            f(lz[:, 1, :], lz[:, 1, :], ACT.Sigmoid).then_inc(S("lora_done"), 1)
            f(lz[0:32, 2, :], lz[0:32, 2, :], ACT.Sigmoid).then_inc(S("lora_done"), 1)

            def qkv_out(e):
                c = 4 * (e // 8) + e % 4
                act.wait_ge(S("w_used"), 4 + UZ + (e if c < 10 else UQ - 1) + 1)
                if c < 8:
                    f(qT[:, c, :], ps[:, c, 0:TOK], ACT.Copy, scale=HD ** -0.5).then_inc(S("qkv_done"), 1)
                elif c < 10:
                    f(kTa[:, c - 8, :], ps[:, c - 8, 0:TOK], ACT.Copy).then_inc(S("qkv_done"), 1)
                else:
                    f(vA[:, c - 10, :], ps[:, c - 8, 0:KV_W], ACT.Copy).then_inc(S("qkv_done"), 1)

            for x in range(UQ + LAG):
                if x < UQ:
                    n, src, shape = q_piece(x)
                    if x % 4 == 0:
                        act.wait_ge(S(f"slot_full{n % RING}"), 16 * (n // RING + 1))
                    buf, used = q_buffer(x)
                    act.wait_ge(S("w_used"), used)
                    f(shape(pieces(buf)[0]), src, ACT.Copy).then_inc(S("w_hi"), 1)
                if x < LAG:
                    z_out(16 - LAG + x, 2)
                elif (x - LAG) % 8 >= 4:
                    qkv_out(x - LAG)

            gate_tile = [0]

            def gate_out():
                q = gate_tile[0]
                gate_tile[0] += 1
                b, t = divmod(q, 2)
                act.wait_ge(*((S("chunk_used"), NG + 2 * b + 2) if t else (S("gate_ps"), b + 1)))
                if q >= 2:
                    act.wait_ge(S(f"gate_stored{t}"), 16 * b)
                f(gtmp[:, t, :], ps[:, 7, :], ACT.Sigmoid).then_inc(S("gate_out"), 1)
                act.wait_ge(S("gate_out"), q + 1)
                act.dma_start(gate_d[:, t, 512 * b:512 * b + 512], gtmp[:, t, :]).then_inc(S(f"gate_stored{t}"), 16)

            for u in range(4):
                n, hg = divmod(u, 2)
                w = 128 * (n + 1)
                if u == 3:
                    gate_out()
                act.wait_ge(S("sm_done"), u + 1)
                f(probs[:, :, 0:w], probs[:, :, 0:w], ACT.Exp).then_inc(S("ex_done"), 1)
                f(aes[:, :], aes[:, :], ACT.Exp).then_inc(S("ex_done"), 1)
                if u == 2:
                    gate_out()
                act.wait_ge(S("pt_ps"), u + 1)
                for kb in range(n + 1):
                    f(probsT[:, kb, :, :], ps[:, 4 - 2 * kb:6 - 2 * kb, :].rearrange("p b (h q) -> p (b h) q", h=4),
                      ACT.Copy).then_inc(S("pt_done"), 1)
                act.wait_ge(S("pv_ps"), u + 1)
                f(attnT[:, 4 * hg:4 * hg + 4, 128 * n:128 * n + 128], ps[:, 0, :].rearrange("p (c q) -> p c q", c=4),
                  ACT.Copy).then_inc(S("pv_done"), 1)
                if u != 2:
                    gate_out()

            for hh in range(HALVES):
                act.wait_ge(S("wl_ps"), hh + 1)
                f(U(4).rearrange("p (b n) -> p b n", b=2), ps[:, 0:2, :], ACT.Sigmoid).then_inc(S("sg_done"), 1)
                act.wait_ge(S("a_ps"), hh + 1)
                for j in range(HJ):
                    last = f(U(5)[:, 256 * j:256 * j + 256], ps[:, 2 + j // 2, 256 * (j % 2):256 * (j % 2) + 256],
                             ACT.Sigmoid, bias=vec("a0", HJ * hh + j))
                last.then_inc(S("a_done"), 1)
                act.wait_ge(S("kkr_done"), hh + 1)
                f(U(7), U(6), ACT.Square).then_inc(S("sq_done"), 1)
                act.wait_ge(S("cum_ps"), hh + 1)
                for bk, g0, gn_ in ((4, 0, 6), (0, 6, 2)):
                    cum = ps[:, bk:bk + gn_ // 2, :].rearrange("p b (t w n) -> p (b t) w n", t=2, w=2)
                    for dst, w, sgn in ((8, 0, 1.0), (9, 0, -1.0), (10, 1, 1.0)):
                        last = f(U(dst).rearrange("p (g n) -> p g n", g=8)[:, g0:g0 + gn_, :], cum[:, :, w, :], ACT.Exp,
                                 scale=sgn * DECAY_C)
                last.then_inc(S("P_done"), 1)
                act.wait_ge(S("ks_ps"), hh + 1)
                f(U(11).rearrange("p (b n) -> p b n", b=2), ps[:, 1:3, :], ACT.Sqrt).then_inc(S("nrm_done"), 1)

                if hh == 0:
                    gate_out()

                def byhead(dst, banks, ev):
                    f(dst, ps[:, banks:banks + 2, :].rearrange("p b (j h x) -> p (b j) h x", j=4, h=2), ACT.Copy)\
                        .then_inc(S(ev), 1)

                def blocks(ap, w):
                    return ap.rearrange("p (h g x) -> p g h x", h=2, g=8, x=w)

                act.wait_ge(S("vtr_ps"), hh + 1)
                byhead(blocks(U(7), 64), 2, "vt2_done")
                gate_out()
                gate_out()
                act.wait_ge(S("at_ps"), hh + 1)
                byhead(blocks(U(4, 2), 128)[:, :, :, 64:128], 4, "at_done")
                act.wait_ge(S("bt_ps"), hh + 1)
                byhead(blocks(U(2), 64), 0, "bt_done")
                act.wait_ge(S("kt_ps"), hh + 1)
                byhead(blocks(U(3), 64), 4, "kt_done")
                act.wait_ge(S("mv_ps"), hh + 1)
                f(U(4, 2).rearrange("p (g x) -> p g x", g=16)[:, :, 0:64],
                  ps[:, 2:4, :].rearrange("p b (g x) -> p (b g) x", g=8), ACT.Copy).then_inc(S("mv_done"), 1)
                for lv in range(1, 6):
                    for hp in range(2):
                        act.wait_ge(S("v1_ps"), 10 * hh + 2 * (lv - 1) + hp + 1)
                        if lv > 1:
                            act.wait_ge(S("wt_ps"), 10 * hh + 2 * (lv - 2) + hp + 1)
                        f(U(14)[:, 512 * hp:512 * hp + 512], ps[:, hp, :], ACT.Copy).then_inc(S("v1_done"), 1)
                    if lv == 5:
                        gate_out()
                act.wait_ge(S("ua_ps"), hh + 1)
                f(U(12, 2).rearrange("p (b n) -> p b n", b=4), ps[:, 2:6, :], ACT.Copy, scale=-1.0)\
                    .then_inc(S("ua_done"), 1)
                act.wait_ge(S("y0_ps"), hh + 1)
                f(U(8).rearrange("p (b n) -> p b n", b=2), ps[:, 0:2, :], ACT.Copy).then_inc(S("y0_done"), 1)
                gate_out()
                act.wait_ge(S("yc_done"), hh + 1)
                f(U(4), U(5), ACT.Square).then_inc(S("ysq_done"), 1)
                act.wait_ge(S("var_done"), hh + 1)
                f(gn[:, 1, :], gn[:, 1, :], ACT.Sqrt).then_inc(S("gsd_done"), 1)
                gate_out()
                if hh == 1:
                    f(m_hi[:, 8:16, :], attnT, ACT.Copy).then_inc(S("m_hi_done"), 1)
                    f(m_hi[:, 0:4, :], yT[:, 0:4, :], ACT.Copy).then_inc(S("m_hi_done"), 1)

            act.wait_ge(S("y_done"), HALVES)
            act.dma_start(x_sb[:, :, :], xv).then_inc(S("x2_in"), 16)
            act.dma_start(rw[:, :, 0:4], a["router_group_w"][0].rearrange("(p k) n -> p k n", p=P)).then_inc(S("rw_in"), 16)
            act.dma_start(rw[:, :, 4:36], a["router_expert_w"][0].rearrange("(p k) n -> p k n", p=P)).then_inc(S("rw_in"), 16)
            assert gate_tile[0] == 16
            f(m_hi[:, 4:8, :], yT[:, 4:8, :], ACT.Copy).then_inc(S("m_hi_done"), 1)
            with act.Fori(0, 2) as i:
                for x in range(16):
                    c, src = v_piece(x)
                    if x % 4 == 0:
                        act.wait_ge(S(f"slot_full{c}"), i * 16 + 16 * (NM // RING + 1))
                    act.wait_ge(S("v_used"), i * 16 + (x + 1))
                    f(late_pieces(x % 4)[0], src, ACT.Copy).then_inc(S("v_hi"), 1)

            def x2_squares(nb):
                act.wait_ge(S("x2_done"), nb + 1)
                for t in range(TT):
                    if nb or t:
                        act.wait_ge(S("sp_done"), TT * nb + t)
                    f(junk3, x_sb[:, t, 512 * nb:512 * nb + 512], ACT.Square, accum_out=sspart[:, 4 * t + nb:4 * t + nb + 1])\
                        .then_inc(S("sp_done"), 1)

            for x in range(UO):
                c, src = v_piece(x)
                if x % 4 == 0:
                    act.wait_ge(S(f"slot_full{c % RING}"), 16 * ((NO + c) // RING + 1))
                act.wait_ge(S("v_used"), UM + x + 1)
                f(late_pieces(x % 4)[0], src, ACT.Copy).then_inc(S("v_hi"), 1)
                if x > 8 and (x - LAG - 1) % 8 == 7:
                    x2_squares((x - LAG - 1) // 8)
                if x == 3:
                    for g in range(8):
                        t, kq = divmod(g, 4)
                        act.wait_ge(S("mtr_ps"), g + 1)
                        f(m_hi[:, 4 * kq:4 * kq + 4, 128 * t:128 * t + 128],
                          ps[:, g, :].rearrange("p (k t) -> p k t", k=4), ACT.Copy).then_inc(S("m_hi_done"), 1)
            act.dma_start(FW, a["final_norm_w"].partition_broadcast(P)).then_inc(S("fw_in"), 16)
            x2_squares(3)
            act.wait_ge(S("ms_done"), 2)
            f(rstd[:, 2:4], rstd[:, 2:4], ACT.Sqrt).then_inc(S("rt_done"), 1)
            for g in range(0, 8, 2):
                hft_out(act, f, [ACT.Copy], g, "hft_act")
            act.wait_ge(S("rt_in"), 1)
            f(rs[:, 400:408], rs[:, 400:408], ACT.Exp).then_inc(S("rt_ex"), 1)
            act.wait_ge(S("rt_in"), 2)
            f(rs[:, 408:410], rs[:, 408:410], ACT.Exp).then_inc(S("rt_ex"), 1)
            act.sem_inc(S("ys_done"), 1)
            with act.Fori(0, GROUPS) as g:
                act.wait_ge(S("b0_full"), g * 7 + 3)
                f(CTB, ps[:, 6, 0:256], ACT.Copy).then_inc(S("b0_free"), 1)
                act.wait_ge(S("chunk_used"), g * PER_G + (NE + 16))
                f(SG, ps[:, 0, :], ACT.Sigmoid).then_inc(S("sgh_done"), 1)
                act.wait_ge(S("b1_full"), g * 7 + 3)
                f(HIDT.rearrange("p k s -> p (k s)"), ps[:, 7, :], ACT.Copy).then_inc(S("b1_free"), 1)
                act.wait_ge(S("chunk_used"), g * PER_G + (NE + PER_G))
                f(YS.rearrange("p (b n) -> p b n", b=4), ps[:, 2:6, :], ACT.Copy).then_inc(S("ys_done"), 1)
            act.wait_ge(S("b0_free"), 7 * GROUPS + 3)
            act.wait_ge(S("b1_free"), 7 * GROUPS + 3)
            over = act.value_load(flag[0:1, 0:1], min_val=0, max_val=1)
            with act.If(over > 0):
                with act.Fori(0, NEXP) as e:
                    act.wait_ge(S("fb_up_used"), e + 1)
                    for t in range(TT):
                        last = f(fSG[:, 512 * t:512 * t + 512], ps[:, t, :], ACT.Sigmoid, scale=rstd[:, 4 + t:5 + t])
                    last.then_inc(S("fb_sg"), 1)
                    act.wait_ge(S("fb_ht_ps"), e + 1)
                    f(fHT.rearrange("p (b n) -> p b n", b=2), ps[:, 4:6, :], ACT.Copy).then_inc(S("fb_ht"), 1)
                act.wait_ge(S("fb_acc"), TT * NEXP + 1)
                act.nop()
            squares(x_sb, junk2, "ss_done")
            act.wait_ge(S("ms_done"), 3)
            f(rstd[:, 2:4], rstd[:, 2:4], ACT.Sqrt).then_inc(S("rt_done"), 1)

        @block.vector
        def _(dve):
            v = nc.vector
            st = Steps(S("dve_step"))

            def step(ins):
                st.on(ins)
                st.last(dve)

            def inv_rms(r, squared="ss_done", count=2):
                dve.wait_ge(S(squared), count)
                if r == 1:
                    step(v.tensor_reduce(rstd[:, 0:2], sspart.rearrange("p (t n) -> p t n", t=TT), AX.X, ALU.add))
                v.tensor_scalar(rstd[:, 2:4], rstd[:, 0:2], 1.0 / D, NORM_EPS, ALU.mult, ALU.add).then_inc(S("ms_done"), 1)
                dve.wait_ge(S("rt_done"), r + 1)
                step(v.reciprocal(rstd[:, 4:6], rstd[:, 2:4]))

            def evac(dst, scale, ps_ev, ev):
                for g in range(8):
                    t, kq = divmod(g, 4)
                    dve.wait_ge(S(ps_ev), g + 1)
                    o = dst[:, 4 * kq:4 * kq + 4, 128 * t:128 * t + 128]
                    i = ps[:, g, :].rearrange("p (k t) -> p k t", k=4)
                    if scale:
                        v.tensor_tensor(o, i, rep(vec(scale, 4 * kq, 4), 128), ALU.mult).then_inc(S(ev), 1)
                    else:
                        v.tensor_copy(o, i).then_inc(S(ev), 1)

            inv_rms(0)
            for t in range(TT):
                v.tensor_scalar(xn[:, t, :], x_sb[:, t, :], rstd[:, 4 + t:5 + t], None, ALU.mult).then_inc(S("xn_done"), 1)
            dve.wait_ge(S("vt_ps"), 1)
            step(v.tensor_copy(vecT[:, 0:NVEC], ps[:, 0, 0:NVEC]))
            step(v.tensor_scalar(omm[:, :], vec("mix", 0, 27), -1.0, 1.0, ALU.mult, ALU.add))
            v.tensor_scalar(omka[:, :], vec("k_a", 0, 8), -1.0, 1.0, ALU.mult, ALU.add).then_inc(S("vt_done"), 1)
            dve.wait_ge(S("vt_done"), 1)
            evac(hT, "anorm", "xt_ps", "ht_done")
            dve.sem_inc(S("w_used"), 4)
            dve.wait_ge(S("h_hi_done"), 1)
            v.tensor_tensor(h_lo[:, :, :], hT, h_hi[:, :, :].bitcast(F32), ALU.subtract).then_inc(S("h_lo_done"), 1)

            for t, m in enumerate((128, 128, 32)):
                dve.wait_ge(S("za_done"), t + 1)
                v.scalar_tensor_tensor(out=lz[0:m, t, 1:TOK], in0=ps[0:m, 4 + t, 0:TOK - 1], scalar=vec("mix", t)[0:m],
                                       in1=lz[0:m, t, 1:TOK], op0=ALU.mult, op1=ALU.add).then_inc(S("z_done"), 1)
            def z_mix(e, i):
                c = 4 * (e // 8) + e % 4
                dve.wait_ge(S("za_done"), i * 8 + (4 + c))
                z = zT[:, bass.ds(i * 8 + c, 1), 1:TOK].rearrange("p a t -> p (a t)")
                v.scalar_tensor_tensor(out=z, in0=ps[:, c, 0:TOK - 1],
                                       scalar=vecT[:, bass.ds(i * 8 + (VEC["mix"] + 3 + c), 1)],
                                       in1=z, op0=ALU.mult, op1=ALU.add).then_inc(S("z_done"), 1)

            def z_lo(x, i):
                n, src = z_piece(x)
                hi, lo = (o.rearrange("p (k n) -> p k n", k=8) for o in pieces(x % 4))
                dve.wait_ge(S("w_hi"), i * 16 + (x + 1))
                v.tensor_tensor(lo, src, hi.bitcast(F32), ALU.subtract).then_inc(S("w_lo"), 1)
                if x % 4 == 3:
                    dve.wait_ge(S("w_lo"), i * 16 + (x + 1))
                    dve.sem_inc(S("chunk_used"), 1)

            for x in range(LAG):
                z_lo(x, 0)
            with dve.Fori(0, 2) as i:
                for x in range(LAG, 16 + LAG):
                    z_lo(x, i)
                    if (x - LAG) % 8 >= 4:
                        z_mix(x - LAG, i)
            for x in range(LAG, 16):
                z_lo(x, 2)
                if (x - LAG) % 8 >= 4:
                    z_mix(x - LAG, 2)
            for x in range(UQ):
                n, src, shape = q_piece(x)
                hi, lo = (shape(o) for o in pieces(q_buffer(x)[0]))
                dve.wait_ge(S("w_hi"), UZ + x + 1)
                v.tensor_tensor(lo, src, hi.bitcast(F32), ALU.subtract).then_inc(S("w_lo"), 1)
                if x % 4 == 3:
                    dve.wait_ge(S("w_lo"), UZ + x + 1)
                    dve.sem_inc(S("chunk_used"), 1)
                if x < LAG:
                    z_mix(16 - LAG + x, 2)
            dve.wait_ge(S("z_done"), 27)

            dve.wait_ge(S("small_in"), 16 * 7)
            for u in range(4):
                n, hg = divmod(u, 2)
                w = 128 * (n + 1)
                sc = ps[:, 0:4, :].rearrange("p b (j k) -> p (b j) k", j=2)
                dve.wait_ge(S("sc_ps"), u + 1)
                for h in range(8):
                    head = 8 * hg + h
                    slope = 2.0 ** (-8.0 * (head + 1) / QH)
                    last = v.scalar_tensor_tensor(out=probs[:, h, 0:w], in0=C("dist", w, 256 - w), scalar=-slope,
                                                  in1=sc[:, h, 0:w], op0=ALU.mult, op1=ALU.add)
                step(last)
                step(v.tensor_reduce(amax[:, :], probs[:, :, 0:w], AX.X, ALU.max))
                step(v.tensor_tensor(amax[:, :], amax[:, :], sink[:, 8 * hg:8 * hg + 8], ALU.max))
                step(v.tensor_tensor(aes[:, :], sink[:, 8 * hg:8 * hg + 8], amax[:, :], ALU.subtract))
                v.tensor_tensor(probs[:, :, 0:w], probs[:, :, 0:w], rep(amax[:, :], w), ALU.subtract)\
                    .then_inc(S("sm_done"), 1)
                dve.wait_ge(S("ex_done"), 2 * u + 2)
                step(v.tensor_reduce(asum[:, :], probs[:, :, 0:w], AX.X, ALU.add))
                step(v.tensor_tensor(asum[:, :], asum[:, :], aes[:, :], ALU.add))
                step(v.reciprocal(asum[:, :], asum[:, :]))
                v.tensor_tensor(probs[:, :, 0:w], probs[:, :, 0:w], rep(asum[:, :], w), ALU.mult)\
                    .then_inc(S("pr_done"), 1)
            dve.wait_ge(S("pv_ps"), 4)

            for hh in range(HALVES):
                def ch(ap):
                    return ap.rearrange("p (j t) -> p j t", j=HJ)

                def g16(ap):
                    return ap.rearrange("p (g x) -> p g x", g=16)

                c0 = HJ * hh
                zr, zk, zv = (zT[:, 8 * w + c0:8 * w + c0 + HJ, :] for w in range(3))
                AR = U(0, 2).rearrange("p (j w t) -> p j w t", j=HJ, w=2)
                if hh:
                    dve.wait_ge(S("y_done"), hh)
                v.tensor_tensor(ch(U(6)), zk, rep(vec("k_k", c0, HJ), TOK), ALU.mult).then_inc(S("kkr_done"), 1)
                dve.wait_ge(S("a_done"), hh + 1)
                for j in range(HJ):
                    last = v.tensor_scalar(ch(U(12))[:, j, :], ch(U(5))[:, j, :], vec("k_a", c0 + j),
                                           omka[:, c0 + j:c0 + j + 1], ALU.mult, ALU.add)
                step(last)
                dve.wait_ge(S("kkr_done"), hh + 1)
                step(v.tensor_tensor(zk, zk, ch(U(12)), ALU.mult))
                step(v.tensor_tensor(ch(U(12)), zr, zk, ALU.mult))
                v.tensor_tensor(ch(U(12)), ch(U(12)), rep(vec("r_k", c0, HJ), TOK), ALU.mult).then_inc(S("rk_done"), 1)
                dve.wait_ge(S("nrm_done"), hh + 1)
                step(v.tensor_scalar(U(11), U(11), 1e-12, None, ALU.max))
                step(v.reciprocal(U(11), U(11)))
                step(v.tensor_tensor(U(6), U(6), U(11), ALU.mult))
                dve.wait_ge(S("P_done"), hh + 1)
                v.tensor_tensor(AR[:, :, 0, :], ch(U(6)), ch(U(10)), ALU.mult)
                v.tensor_tensor(AR[:, :, 1, :], zr, ch(U(8)), ALU.mult)
                step(v.tensor_tensor(U(11), U(6), U(5), ALU.mult))
                v.tensor_tensor(U(2), U(11), U(9), ALU.mult)
                v.tensor_copy(pend[:, :].rearrange("p (b a j) -> p b a j", b=2, a=2),
                              U(8).rearrange("p (j a b t) -> p b a j t", j=HJ, a=2, b=2)[:, :, :, :, 63])
                v.tensor_tensor(ch(U(3)), zk, ch(U(9)), ALU.mult).then_inc(S("arbk"), 1)
                dve.wait_ge(S("arbk"), hh + 1)
                dve.wait_ge(S("bon_ps"), hh + 1)
                v.tensor_tensor(zr, ps[:, 4:6, :].rearrange("p b (j t) -> p (b j) t", j=2), zv, ALU.mult)\
                    .then_inc(S("bon_done"), 1)
                dve.wait_ge(S("l_ps"), hh + 1)
                v.tensor_tensor(g16(U(12)), ps[:, 0:2, :].rearrange("p b (g x) -> p (b g) x", g=8), tile16(C("m1L")),
                                ALU.mult).then_inc(S("x0_done"), 1)
                dve.wait_ge(S("x0_done"), hh + 1)
                v.scalar_tensor_tensor(out=g16(U(12)), in0=g16(U(12)), scalar=-1.0, in1=tile16(C("eye")),
                                       op0=ALU.mult, op1=ALU.add).then_inc(S("x_done"), 2)
                dve.wait_ge(S("lt_ps"), hh + 1)
                lt = ps[:, 2:6, :].rearrange("p b (g w x) -> p (b g) w x", g=4, w=2)
                v.tensor_tensor(g16(U(8)), lt[:, :, 0, :], tile16(C("mU")), ALU.mult)
                v.tensor_tensor(g16(U(9)), lt[:, :, 1, :], tile16(C("mUi")), ALU.mult).then_inc(S("lt_done"), 1)
                dve.wait_ge(S("lt_done"), hh + 1)
                step(v.tensor_tensor(g16(U(14)), g16(U(8)), tile16(C("lvlT", 64)), ALU.mult))
                v.scalar_tensor_tensor(out=g16(U(13)), in0=g16(U(14)), scalar=-1.0, in1=tile16(C("eye")),
                                       op0=ALU.mult, op1=ALU.add).then_inc(S("xt_done"), 2)
                dve.wait_ge(S("mt_ps"), hh + 1)
                mt = ps[:, 0:4, :].rearrange("p b (g w x) -> p (b g) w x", g=4, w=2)
                v.tensor_tensor(g16(U(10)), mt[:, :, 0, :], tile16(C("mU")), ALU.mult)
                v.tensor_tensor(g16(U(11)), mt[:, :, 1, :], tile16(C("mUi")), ALU.mult).then_inc(S("mt_done"), 1)
                for lv in range(1, 6):
                    for w, ev in ((0, "w_ps"), (1, "wt_ps"))[lv == 5:]:
                        for hp in range(2):
                            dve.wait_ge(S(ev), (8, 10)[w] * hh + 2 * (lv - 1) + hp + 1)
                            x = U(12 + w)[:, 512 * hp:512 * hp + 512]
                            if w:
                                dve.wait_ge(S("xt_done"), 12 * hh + 2 * (lv - 1) + hp + 1)
                            else:
                                dve.wait_ge(S("x_done"), 10 * hh + 2 * (lv - 1) + hp + 1)
                            v.tensor_tensor(x, x, ps[:, 2 + 2 * w + hp, :], ALU.subtract)\
                                .then_inc(S(("x_done", "xt_done")[w]), 1)
                dve.wait_ge(S("rb_ps"), hh + 1)
                for cp in range(2):
                    for ci in range(2):
                        rt = AR[:, :, 1, 128 * ci + 64 * cp:128 * ci + 64 * cp + 64]
                        last = v.tensor_tensor(rt, rt, ps[:, cp, 256 * ci:256 * ci + 256].rearrange(
                            "p (j x) -> p j x", j=HJ), ALU.add)
                last.then_inc(S("rb_done"), 1)
                dve.wait_ge(S("g_ps"), hh + 1)
                v.tensor_tensor(g16(U(10)), ps[:, 2:4, :].rearrange("p b (g x) -> p (b g) x", g=8), tile16(C("eye")),
                                ALU.add).then_inc(S("g_done"), 1)
                dve.wait_ge(S("f_ps"), hh + 1)
                v.tensor_tensor(g16(U(14)), ps[:, 4:6, :].rearrange("p b (g x) -> p (b g) x", g=8),
                                rep(pend[:, :], 64), ALU.mult).then_inc(S("f_done"), 1)
                dve.wait_ge(S("f_done"), hh + 1)
                for c in (1, 2):
                    ci, cp = divmod(c, 2)
                    o = 8 * cp + 4 * ci
                    s = U(6)[:, 256 * (c - 1):256 * c]
                    dve.wait_ge(S("s_ps"), 2 * hh + c)
                    step(v.tensor_tensor(s.rearrange("p (j x) -> p j x", j=HJ),
                                         ps[:, 6, 256 * (c - 1):256 * c].rearrange("p (j x) -> p j x", j=HJ),
                                         rep(pend[:, o:o + 4], 64), ALU.mult))
                    v.tensor_tensor(s, s, U(14)[:, 64 * o:64 * o + 256], ALU.add).then_inc(S("s_done"), 1)
                dve.wait_ge(S("yy_ps"), hh + 1)
                dve.wait_ge(S("y0_done"), hh + 1)
                Y = U(8)
                y2 = Y.rearrange("p (h n) -> p h n", h=2)
                step(v.tensor_tensor(y2[64:128], y2[64:128], ps[64:128, 2:4, :], ALU.add))
                step(v.tensor_tensor(y2[0:64, :, 256:512], y2[0:64, :, 256:512], ps[0:64, 2:4, 256:512], ALU.add))
                step(v.tensor_reduce(gn[:, 0, :], g16(Y), AX.X, ALU.add))
                step(v.tensor_scalar(gn[:, 0, :], gn[:, 0, :], 1.0 / HD, None, ALU.mult))
                v.tensor_tensor(g16(U(5)), g16(Y), rep(gn[:, 0, :], 64), ALU.subtract).then_inc(S("yc_done"), 1)
                dve.wait_ge(S("ysq_done"), hh + 1)
                step(v.tensor_reduce(gn[:, 1, :], g16(U(4)), AX.X, ALU.add))
                v.tensor_scalar(gn[:, 1, :], gn[:, 1, :], 1.0 / HD, GN_EPS, ALU.mult, ALU.add).then_inc(S("var_done"), 1)
                dve.wait_ge(S("gsd_done"), hh + 1)
                step(v.reciprocal(gn[:, 2, :], gn[:, 1, :]))
                for hp in range(2):
                    last = v.tensor_tensor(U(4).rearrange("p (g h x) -> p g h x", g=8, h=2)[:, :, hp, :],
                                           U(5)[:, 512 * hp:512 * hp + 512].rearrange("p (g x) -> p g x", g=8),
                                           rep(gn[:, 2, 8 * hp:8 * hp + 8], 64), ALU.mult)
                last.then_inc(S("yn_done"), 1)
                if hh == 1:
                    for h, (dst, src) in enumerate(((slice(8, 16), attnT), (slice(0, 4), yT[:, 0:4, :]))):
                        dve.wait_ge(S("m_hi_done"), h + 1)
                        v.tensor_tensor(m_lo[:, dst, :], src, m_hi[:, dst, :].bitcast(F32), ALU.subtract)\
                            .then_inc(S("m_lo_done"), 1)
                dve.wait_ge(S("ynt_ps"), hh + 1)
                for j in range(HJ):
                    last = v.tensor_scalar(ch(U(5))[:, j, :], ps[:, j // 2, 256 * (j % 2):256 * (j % 2) + 256],
                                           vec("ln_w", c0 + j), vec("ln_b", c0 + j), ALU.mult, ALU.add)
                step(last)
                dve.wait_ge(S("bon_done"), hh + 1)
                step(v.tensor_tensor(ch(U(5)), ch(U(5)), zr, ALU.add))
                dve.wait_ge(S("gt_ps"), hh + 1)
                v.tensor_tensor(zv, ch(U(5)), ps[:, 4:6, :].rearrange("p b (j t) -> p (b j) t", j=2), ALU.mult)\
                    .then_inc(S("y_done"), 1)

            dve.sem_inc(S("v_used"), 3)
            dve.wait_ge(S("m_hi_done"), 3)
            v.tensor_tensor(m_lo[:, 4:8, :], yT[:, 4:8, :], m_hi[:, 4:8, :].bitcast(F32), ALU.subtract)\
                .then_inc(S("m_lo_done"), 1)
            dve.wait_ge(S("m_lo_done"), 3)
            dve.sem_inc(S("v_used"), 1)
            dve.sem_inc(S("m1_done"), 1)
            dve.sem_inc(S("m2_done"), 1)

            def v_lo(x, hi_count, lo_count):
                hi, lo = late_pieces(x % 4)
                dve.wait_ge(S("v_hi"), hi_count)
                v.tensor_tensor(lo, v_piece(x)[1], hi.bitcast(F32), ALU.subtract).then_inc(S("v_lo"), 1)
                if x % 4 == 3:
                    dve.wait_ge(S("v_lo"), lo_count)
                    dve.sem_inc(S("chunk_used"), 1)

            def gated(c):
                nb, g = divmod(c, 2)
                b = nb % 2
                if g == 0:
                    dve.wait_ge(S(f"gate_in{b}"), nb // 2 * 32 + 32)
                dve.wait_ge(S("v_used"), 4 + 4 * c + 4)
                v.tensor_tensor(gates[b][g], gates[b][g], ps[:, 2 * g:2 * g + 2, :], ALU.mult)\
                    .then_inc(S(("m1_done", "m2_done")[g]), 1)
                if g:
                    dve.wait_ge(S("m1_done"), nb + 2)
                    dve.wait_ge(S("m2_done"), nb + 2)
                    v.tensor_tensor(mg[:, :, 512 * nb:512 * nb + 512], gates[b][0], gates[b][1], ALU.add)\
                        .then_inc(S("mg_done"), 1)

            for x in range(UM):
                v_lo(x, x + 1, x + 1)
                if x >= 4 + LAG - 1 and (x - LAG) % 4 == 3:
                    gated((x - LAG) // 4)
            gated(7)

            def x2(nb):
                dve.wait_ge(S("v_used"), 4 + UM + 8 * nb + 8)
                xs = x_sb[:, :, 512 * nb:512 * nb + 512]
                v.tensor_tensor(xs, xs, ps[:, 2 * nb:2 * nb + 2, :], ALU.add).then_inc(S("x2_done"), 1)

            dve.wait_ge(S("rw_in"), 32)
            v.tensor_tensor(rw, rw, rep(fnorm[:, :], 36), ALU.mult).then_inc(S("rw_scaled"), 1)
            dve.wait_ge(S("x2_in"), 16)
            for x in range(UO):
                v_lo(x, UM + x + 1, UM + x + 1)
                if x == 3:
                    for g in range(8):
                        t, kq = divmod(g, 4)
                        o = (slice(0, P), slice(4 * kq, 4 * kq + 4), slice(128 * t, 128 * t + 128))
                        dve.wait_ge(S("m_hi_done"), 3 + g + 1)
                        v.tensor_tensor(m_lo[o], ps[:, g, :].rearrange("p (k t) -> p k t", k=4), m_hi[o].bitcast(F32),
                                        ALU.subtract).then_inc(S("m_lo_done"), 1)
                if x > 8 and (x - LAG) % 8 == 7:
                    x2((x - LAG) // 8)
            x2(3)
            dve.wait_ge(S("x2_done"), 4)
            inv_rms(1, "sp_done", 8)
            for t in range(TT):
                v.tensor_scalar(hfn[:, t, :].rearrange("q (k p) -> q k p", k=KT),
                                x_sb[:, t, :].rearrange("q (p k) -> q k p", k=KT), rstd[:, 4 + t:5 + t], None, ALU.mult).then_inc(S("hfn_done"), 1)
            for g in range(1, 8, 2):
                hft_out(dve, v.tensor_copy, [], g, "hft_dve")

            def R(at, n, w=None):
                r = rs[:, at:at + TT * n]
                return r.rearrange("p (a n) -> p a n", a=TT)

            AM, WT, POS, WOV = R(0, 32), R(64, 32), R(128, 32), R(192, 32)
            LG, EL, EQ, OH1 = R(256, 36), R(416, 32), R(480, 32), R(544, 32)
            GX, EX = R(400, 4), rs[:, 408:410]
            GM, GI, GOH, GS = rs[:, 608:610], rs[:, 610:612], R(612, 4), rs[:, 620:622]
            M1, M2, MI, W1, W2 = (rs[:, 622 + 2 * i:624 + 2 * i] for i in range(5))
            CNT = rs[:, 640:641]
            TMP = R(648, 32)
            iota = C("iota")
            dve.wait_ge(S("lg_ps"), 1)
            dve.wait_ge(S("rb_in"), 16)

            def both(ap, n):
                return ap.unsqueeze(1).to_broadcast([P, TT, n])

            for t in range(TT):
                last = v.scalar_tensor_tensor(out=LG[:, t, :], in0=ps[:, t, 0:36], scalar=rstd[:, 4 + t:5 + t],
                                              in1=rbias[:, :], op0=ALU.mult, op1=ALU.add)
            step(last)
            gl = LG[:, :, 0:4]
            step(v.tensor_reduce(GM, gl, AX.X, ALU.max))
            v.tensor_tensor(GX, gl, rep(GM, 4), ALU.subtract).then_inc(S("rt_in"), 1)
            step(v.tensor_tensor(GOH, gl, rep(GM, 4), ALU.is_equal))
            step(v.scalar_tensor_tensor(out=GOH, in0=GOH, scalar=-64.0, in1=both(iota[:, 0:4], 4), op0=ALU.mult, op1=ALU.add))
            step(v.tensor_reduce(GI, GOH, AX.X, ALU.min))
            step(v.tensor_tensor(GOH, GOH, rep(GI, 4), ALU.is_equal))
            step(v.tensor_scalar(GOH, GOH, 1.0, BIG, ALU.subtract, ALU.mult))
            step(v.tensor_copy(EL, LG[:, :, 4:36]))
            el8 = rs[:, 416:480].rearrange("p (g e) -> p g e", g=8)
            step(v.tensor_tensor(el8, el8, rep(rs[:, 612:620], 8), ALU.add))

            def first_best(m, oh):
                step(v.tensor_reduce(m, EL, AX.X, ALU.max))
                step(v.tensor_tensor(oh, EL, rep(m, 32), ALU.is_equal))
                step(v.scalar_tensor_tensor(out=oh, in0=oh, scalar=-64.0, in1=both(iota, 32), op0=ALU.mult, op1=ALU.add))
                step(v.tensor_reduce(MI, oh, AX.X, ALU.min))
                step(v.tensor_tensor(oh, oh, rep(MI, 32), ALU.is_equal))

            first_best(M1, OH1)
            step(v.scalar_tensor_tensor(out=EL, in0=OH1, scalar=-3 * BIG, in1=EL, op0=ALU.mult, op1=ALU.add))
            first_best(M2, EQ)
            v.tensor_tensor(EX, M2, M1, ALU.subtract).then_inc(S("rt_in"), 1)
            v.tensor_tensor(AM, OH1, EQ, ALU.add).then_inc(S("picks"), 1)
            dve.wait_ge(S("rt_ex"), 2)
            step(v.tensor_reduce(GS, GX, AX.X, ALU.add))
            step(v.tensor_scalar(W1, EX, 1.0, None, ALU.add))
            step(v.tensor_tensor(W1, W1, GS, ALU.mult))
            step(v.reciprocal(W1, W1))
            step(v.tensor_tensor(W2, EX, W1, ALU.mult))
            step(v.tensor_tensor(OH1, OH1, rep(W1, 32), ALU.mult))
            step(v.tensor_tensor(EQ, EQ, rep(W2, 32), ALU.mult))
            step(v.tensor_tensor(WT, OH1, EQ, ALU.add))
            dve.wait_ge(S("pos_ps"), 1)
            dve.wait_ge(S("picks"), 1)
            step(v.tensor_scalar(TMP, ps[:, 2:4, 0:32], float(CAP), None, ALU.is_ge))
            step(v.tensor_tensor(WOV, TMP, WT, ALU.mult))
            step(v.tensor_scalar(POS, ps[:, 2:4, 0:32], 1.0, None, ALU.add))
            step(v.tensor_tensor(POS, POS, AM, ALU.mult))
            step(v.tensor_scalar(POS, POS, -1.0, None, ALU.add))
            step(v.tensor_reduce(CNT, ps[:, 4, 0:32], AX.X, ALU.max))
            v.tensor_scalar(flag[0:1, 0:1], CNT[0:1], CAP + 0.5, None, ALU.is_ge).then_inc(S("flag_set"), 1)

            for ev in ("b0_free", "b1_free", "hid_done"):
                dve.sem_inc(S(ev), 1)

            def one_hots(where):
                for t in range(TT):
                    o = OH[:, 128 * t:128 * t + 128].rearrange("p (j s) -> p j s", j=GE)
                    last = v.tensor_tensor(o, iota.unsqueeze(1).to_broadcast([P, GE, CAP]),
                                           rep(rs[:, where(128 + 32 * t)], CAP), ALU.is_equal)
                step(last)
                for t in range(TT):
                    o = OH[:, 128 * t:128 * t + 128].rearrange("p (j s) -> p j s", j=GE)
                    ow = OHW[:, 128 * t:128 * t + 128].rearrange("p (j s) -> p j s", j=GE)
                    last = v.tensor_tensor(ow, o, rep(rs[:, where(64 + 32 * t)], CAP), ALU.mult)
                last.then_inc(S("oh_done"), 1)

            def gathered(q):
                v.tensor_tensor(XS[:, 4 * q:4 * q + 4, :], ps[:, 6 + q % 2, :].rearrange("p (k s) -> p k s", k=4),
                                rep(vec("fnorm", 4 * q, 4), 128), ALU.mult).then_inc(S(f"b{q % 2}_free"), 1)

            one_hots(lambda at: slice(at, at + GE))
            for q in range(4):
                dve.wait_ge(S(f"b{q % 2}_full"), q // 2 + 1)
                gathered(q)
            with dve.Fori(0, GROUPS) as g:
                st.enter(g, 2)
                dve.wait_ge(S("b0_full"), g * 7 + 3)
                one_hots(lambda at: bass.ds(g * GE + (at + GE), GE))
                dve.wait_ge(S("sgh_done"), g + 1)
                step(v.tensor_tensor(HIDB, SG, ps[:, 0, :], ALU.mult))
                v.tensor_tensor(HIDB, HIDB, ps[:, 1, :], ALU.mult).then_inc(S("hid_done"), 1)
                for q in range(4):
                    dve.wait_ge(S(f"b{q % 2}_full"), g * 7 + (4 + q // 2))
                    gathered(q)
                for u in range(8):
                    t, nb = divmod(u, 4)
                    dve.wait_ge(S(f"b{u % 2}_full"), g * 7 + (6 + u // 2))
                    xs = x_sb[:, t, 512 * nb:512 * nb + 512]
                    last = v.tensor_tensor(xs, xs, ps[:, 6 + u % 2, :], ALU.add)
                    last.then_inc(S(f"b{u % 2}_free"), 1)
            st.leave(GROUPS)
            over = dve.value_load(flag[0:1, 0:1], min_val=0, max_val=1)
            dve.wait_ge(S("b0_free"), 7 * GROUPS + 3)
            dve.wait_ge(S("b1_free"), 7 * GROUPS + 3)
            with dve.If(over > 0):
                v.tensor_tensor(hfT, hfT, rep(fnorm[:, :], TOK), ALU.mult).then_inc(S("fb_acc"), 1)
                with dve.Fori(0, NEXP) as e:
                    dve.wait_ge(S("fb_sg"), e + 1)
                    for w, src, ev in ((0, fSG, "fb_silu"), (1, fHID, "fb_hid")):
                        if w:
                            dve.wait_ge(S("fb_silu"), e + 1)
                        for t in range(TT):
                            o = slice(512 * t, 512 * t + 512)
                            last = v.scalar_tensor_tensor(out=fHID[:, o], in0=ps[:, 2 * w + t, :],
                                                          scalar=rstd[:, 4 + t:5 + t], in1=src[:, o],
                                                          op0=ALU.mult, op1=ALU.mult)
                        last.then_inc(S(ev), 1)
                    for t in range(TT):
                        dve.wait_ge(S("fb_dn_ps"), e * 2 + (t + 2))
                        xs = x_sb[:, t, :].rearrange("p (b n) -> p b n", b=4)
                        v.scalar_tensor_tensor(out=xs, in0=ps[:, 4 * t:4 * t + 4, :],
                                               scalar=rs[:, bass.ds(e + (192 + 32 * t), 1)], in1=xs,
                                               op0=ALU.mult, op1=ALU.add).then_inc(S("fb_acc"), 1)
                        dve.wait_ge(S("fb_acc"), e * 2 + (t + 2))
                dve.nop()
            inv_rms(2, "ss_done", 4)
            dve.wait_ge(S("fw_in"), 16)
            for t in range(TT):
                v.scalar_tensor_tensor(out=fout[:, t, :], in0=x_sb[:, t, :], scalar=rstd[:, 4 + t:5 + t], in1=FW,
                                       op0=ALU.mult, op1=ALU.mult).then_inc(S("fin"), 1)


_INS = ["x", "attn_norm_w", "w_in", "shift_mix", "attn_sinks", "rwkv_w0", "rwkv_w_up", "rwkv_a0", "rwkv_a_up",
        "rwkv_g_up", "rwkv_k_k", "rwkv_k_a", "rwkv_r_k", "rwkv_ln_w", "rwkv_ln_b", "w_branch_a", "w_branch_b",
        "w_out", "ffn_norm_w", "router_group_w", "router_group_b", "router_expert_w", "router_expert_b",
        "expert_w_gate", "expert_w_up", "expert_w_down", "final_norm_w"]


def kernel(**inputs):
    import numpy as _np
    import concourse.bacc as _bacc
    from concourse import mybir as _mybir
    from concourse.bass_utils import run_bass_kernel_spmd as _run

    nc = _bacc.Bacc("TRN2", target_bir_lowering=False, num_devices=1)
    arrays, aps = {}, {}
    for name in _INS:
        arrays[f"in_{name}"] = _np.ascontiguousarray(inputs[name])
    arrays["in_consts"] = constants()
    for key, arr in arrays.items():
        aps[key[3:]] = nc.dram_tensor(key, arr.shape, _mybir.dt.from_np(arr.dtype), kind="ExternalInput").ap()
    out = nc.dram_tensor("out", (1, TOK, D), F32, kind="ExternalOutput").ap()
    hybrid_layer(nc, aps, out)
    r = _run(nc, [arrays], core_ids=[0])
    return r.results[0]["out"]
```
